# Optimizing a Trainium2 kernel written in Bass

```python
import jax, jax.numpy as jnp
from jax import lax
import numpy as np

D_MODEL = 1024
BATCH = 1
SEQ = 512
DEPTH = 1

A_HEADS = 8
A_HEAD_DIM = 64
A_WIDTH = A_HEADS * A_HEAD_DIM
Q_LORA_RANK = 256
IDX_HEADS = 4
IDX_DIM = 64
TOPK_MAX = 256
Q_BLOCK = 128
B_WIDTH = 512
B_EXPAND = 128
B_HEADS = B_WIDTH // B_EXPAND
B_HEAD_V = B_WIDTH // B_HEADS
CHUNK = 16
D_FF = 4 * D_MODEL
EPS = 1e-6

COL_SIZES = (Q_LORA_RANK, A_WIDTH, A_WIDTH, IDX_DIM, IDX_HEADS,
             B_WIDTH, B_WIDTH, B_WIDTH, B_WIDTH, D_MODEL, D_MODEL)
D_IN = sum(COL_SIZES)

kernel_name = 'hybrid_dsa_hgrn2_gated_block'

def rms_norm(x, g):
    xf = x.astype(jnp.float32)
    y = xf * lax.rsqrt(jnp.mean(xf * xf, axis=-1, keepdims=True) + EPS)
    return (y * g.astype(jnp.float32)).astype(x.dtype)

def split_cols(t, sizes):
    points, acc = [], 0
    for s in sizes[:-1]:
        acc += s
        points.append(acc)
    return jnp.split(t, points, axis=-1)

def dsa_attention(q, k, v, q_idx, k_idx, w_idx):
    B, L = q.shape[0], q.shape[1]
    topk = min(TOPK_MAX, L // 4)
    nblk = L // Q_BLOCK
    key_pos = jnp.arange(L)
    scale = A_HEAD_DIM ** -0.5
    idx_scale = (IDX_DIM ** -0.5) * (IDX_HEADS ** -0.5)
    k_idx_f = k_idx.astype(jnp.float32)

    def to_blocks(t):
        return t.reshape((B, nblk, Q_BLOCK) + t.shape[2:]).swapaxes(0, 1)

    def block(args):
        qb, qib, wb, start = args
        q_pos = start + jnp.arange(Q_BLOCK)
        causal = key_pos[None, :] <= q_pos[:, None]
        rel = jax.nn.relu(jnp.einsum('bthd,bsd->bths', qib.astype(jnp.float32), k_idx_f))
        score = jnp.einsum('bth,bths->bts', wb.astype(jnp.float32) * idx_scale, rel)
        score = jnp.where(causal[None], score, -jnp.inf)
        top_val, top_idx = lax.top_k(score, topk)
        valid = top_val > -jnp.inf
        kg = jax.vmap(lambda kb, ib: kb[ib])(k, top_idx)
        vg = jax.vmap(lambda vb, ib: vb[ib])(v, top_idx)
        logits = jnp.einsum('bthd,btkhd->bhtk', qb.astype(jnp.float32), kg.astype(jnp.float32)) * scale
        logits = jnp.where(valid[:, None], logits, -jnp.inf)
        p = jax.nn.softmax(logits, axis=-1)
        o = jnp.einsum('bhtk,btkhd->bthd', p, vg.astype(jnp.float32))
        return o.astype(q.dtype)

    starts = jnp.arange(nblk) * Q_BLOCK
    out = lax.map(block, (to_blocks(q), to_blocks(q_idx), to_blocks(w_idx), starts))
    return out.swapaxes(0, 1).reshape(B, L, A_WIDTH)

def hgrn2_chunkwise(q, f_logit, i, lb):
    B, L, H, dk = q.shape
    dv = i.shape[-1]
    n = L // CHUNK
    lbh = lb.reshape(H, dk).astype(jnp.float32)
    f = lbh + (1.0 - lbh) * jax.nn.sigmoid(f_logit.astype(jnp.float32))
    k = 1.0 - f
    log_f = jnp.log(f)

    def chunks(t):
        return t.reshape(B, n, CHUNK, H, t.shape[-1])

    qc, kc, vc, gc = chunks(q.astype(jnp.float32)), chunks(k), chunks(i.astype(jnp.float32)), chunks(log_f)
    b = jnp.cumsum(gc, axis=2)
    b_end = b[:, :, -1]
    causal = jnp.tril(jnp.ones((CHUNK, CHUNK), dtype=bool))
    diff = b[:, :, :, None] - b[:, :, None, :]
    decay = jnp.exp(jnp.where(causal[None, None, :, :, None, None], diff, -jnp.inf))
    attn = jnp.einsum('bnthd,bnshd,bntshd->bnhts', qc, kc, decay)
    o_intra = jnp.einsum('bnhts,bnshv->bnthv', attn, vc)
    kv = jnp.einsum('bnshd,bnshv->bnhdv', kc * jnp.exp(b_end[:, :, None] - b), vc)

    def step(S, inp):
        dec, upd = inp
        return dec[..., None] * S + upd, S

    S0 = jnp.zeros((B, H, dk, dv), jnp.float32)
    _, S_prev = lax.scan(step, S0, (jnp.exp(b_end).swapaxes(0, 1), kv.swapaxes(0, 1)))
    S_prev = S_prev.swapaxes(0, 1)
    o_inter = jnp.einsum('bnthd,bnhdv->bnthv', qc * jnp.exp(b), S_prev)
    return (o_intra + o_inter).reshape(B, L, H, dv)

def setup_inputs(seed: int = 0) -> dict:
    key = jax.random.key(seed)
    ks = jax.random.split(key, 24)
    f32 = jnp.float32

    def nrm(k, shape, fan_in):
        return jax.random.normal(k, shape, f32) * (fan_in ** -0.5)

    def gain(k, shape):
        return 1.0 + 0.05 * jax.random.normal(k, shape, f32)

    def bias(k, shape, s=0.01):
        return s * jax.random.normal(k, shape, f32)

    return {
        'x': jax.random.normal(ks[0], (BATCH, SEQ, D_MODEL), f32),
        'c': jax.random.normal(ks[1], (BATCH, D_MODEL), f32),
        'w_ada': nrm(ks[2], (DEPTH, D_MODEL, 6 * D_MODEL), D_MODEL),
        'b_ada': bias(ks[3], (DEPTH, 6 * D_MODEL), 0.02),
        'norm1_g': gain(ks[4], (DEPTH, D_MODEL)),
        'w_in': nrm(ks[5], (DEPTH, D_MODEL, D_IN), D_MODEL),
        'q_lat_norm_g': gain(ks[6], (DEPTH, Q_LORA_RANK)),
        'w_uq': nrm(ks[7], (DEPTH, Q_LORA_RANK, A_WIDTH), Q_LORA_RANK),
        'w_uq_idx': nrm(ks[8], (DEPTH, Q_LORA_RANK, IDX_HEADS * IDX_DIM), Q_LORA_RANK),
        'q_norm_g': gain(ks[9], (DEPTH, A_HEAD_DIM)),
        'k_norm_g': gain(ks[10], (DEPTH, A_HEAD_DIM)),
        'k_idx_norm_g': gain(ks[11], (DEPTH, IDX_DIM)),
        'hgrn_lb': 0.5 * jax.random.normal(ks[12], (DEPTH + 1, B_WIDTH), f32),
        'hgrn_o_norm_g': gain(ks[13], (DEPTH, B_WIDTH)),
        'w_proj_a': nrm(ks[14], (DEPTH, A_WIDTH, D_MODEL), A_WIDTH),
        'w_proj_b': nrm(ks[15], (DEPTH, B_WIDTH, D_MODEL), B_WIDTH),
        'w_out': nrm(ks[16], (DEPTH, D_MODEL, D_MODEL), D_MODEL),
        'norm2_g': gain(ks[17], (DEPTH, D_MODEL)),
        'w_mlp1': nrm(ks[18], (DEPTH, D_MODEL, D_FF), D_MODEL),
        'b_mlp1': bias(ks[19], (DEPTH, D_FF)),
        'w_mlp2': nrm(ks[20], (DEPTH, D_FF, D_MODEL), D_FF),
        'b_mlp2': bias(ks[21], (DEPTH, D_MODEL)),
    }

def reference(x, c, w_ada, b_ada, norm1_g, w_in, q_lat_norm_g, w_uq, w_uq_idx, q_norm_g, k_norm_g,
              k_idx_norm_g, hgrn_lb, hgrn_o_norm_g, w_proj_a, w_proj_b, w_out, norm2_g,
              w_mlp1, b_mlp1, w_mlp2, b_mlp2):
    B, L = x.shape[0], x.shape[1]
    lb_all = jnp.cumsum(jax.nn.softmax(hgrn_lb.astype(jnp.float32), axis=0), axis=0)
    c_act = jax.nn.silu(c)
    for l in range(DEPTH):
        mod = c_act @ w_ada[l] + b_ada[l]
        shift1, scale1, gate1, shift2, scale2, gate2 = jnp.split(mod, 6, axis=-1)

        h = rms_norm(x, norm1_g[l]) * (1.0 + scale1[:, None]) + shift1[:, None]
        proj = h @ w_in[l]
        (q_lat, a_k, a_v, k_idx, w_idx, b_q, b_f, b_i, b_g, gate_a, gate_b) = split_cols(proj, COL_SIZES)

        q_lat = rms_norm(q_lat, q_lat_norm_g[l])
        a_q = rms_norm((q_lat @ w_uq[l]).reshape(B, L, A_HEADS, A_HEAD_DIM), q_norm_g[l])
        a_k = rms_norm(a_k.reshape(B, L, A_HEADS, A_HEAD_DIM), k_norm_g[l])
        a_v = a_v.reshape(B, L, A_HEADS, A_HEAD_DIM)
        q_idx = (q_lat @ w_uq_idx[l]).reshape(B, L, IDX_HEADS, IDX_DIM)
        k_idx = rms_norm(k_idx, k_idx_norm_g[l])
        out_a = dsa_attention(a_q, a_k, a_v, q_idx, k_idx, w_idx)

        hq = jax.nn.silu(b_q).reshape(B, L, B_HEADS, B_EXPAND)
        hf = b_f.reshape(B, L, B_HEADS, B_EXPAND)
        hi = b_i.reshape(B, L, B_HEADS, B_HEAD_V)
        o_b = hgrn2_chunkwise(hq, hf, hi, lb_all[l]).astype(x.dtype)
        o_b = rms_norm(o_b, hgrn_o_norm_g[l].reshape(B_HEADS, B_HEAD_V)).reshape(B, L, B_WIDTH)
        out_b = o_b * jax.nn.silu(b_g)

        merged = jax.nn.sigmoid(gate_a) * (out_a @ w_proj_a[l]) + jax.nn.sigmoid(gate_b) * (out_b @ w_proj_b[l])
        x = x + gate1[:, None] * (merged @ w_out[l])

        h2 = rms_norm(x, norm2_g[l]) * (1.0 + scale2[:, None]) + shift2[:, None]
        y = jnp.square(jax.nn.relu(h2 @ w_mlp1[l] + b_mlp1[l])) @ w_mlp2[l] + b_mlp2[l]
        x = x + gate2[:, None] * y
    return x


_drawn_inputs = setup_inputs


def setup_inputs(seed=0):
    import zlib

    import numpy as np

    out = dict(_drawn_inputs(seed))
    spreads = {}
    factors = {'norm1_g': 3.087,
     'q_lat_norm_g': 7.025,
     'q_norm_g': 8.0,
     'k_norm_g': 8.0,
     'k_idx_norm_g': 7.707,
     'hgrn_lb': 5.504,
     'hgrn_o_norm_g': 4.594,
     'b_mlp1': 25.038,
     'b_mlp2': 199.248,
     'norm2_g': 4.742}
    for name, (base, spread) in spreads.items():
        noise = np.random.default_rng([zlib.crc32(name.encode()), seed]).standard_normal(out[name].shape)
        drawn = base * np.exp(spread * noise) if base else spread * noise
        out[name] = __import__('jax').numpy.asarray(drawn.astype(out[name].dtype))
    for name, factor in factors.items():
        out[name] = (out[name] * factor).astype(out[name].dtype)
    return out
```

```python
from contextlib import ExitStack

import concourse.bass as bass
from concourse import mybir

F32 = mybir.dt.float32
F32R = mybir.dt.float32r
I8 = mybir.dt.int8
ALU = mybir.AluOpType
ACT = mybir.ActivationFunctionType

P = 128
WS = 4
EPS = 1e-6
MASKED = -3.0e38
TAKEN = -3.4028235e38
TAKEN_BELOW = -3.3e38
FORBID = -1.0e30


def hybrid_block(nc, x, c, w_ada, b_ada, norm1_g, w_in, q_lat_norm_g, w_uq, w_uq_idx, q_norm_g,
                 k_norm_g, k_idx_norm_g, hgrn_lb, hgrn_o_norm_g, w_proj_a, w_proj_b, w_out,
                 norm2_g, w_mlp1, b_mlp1, w_mlp2, b_mlp2, out):
    T, D = x.shape[1], x.shape[2]
    KC = D // P
    TB = T // P
    R = q_lat_norm_g.shape[1]
    AW = w_proj_a.shape[1]
    HD = q_norm_g.shape[1]
    AH = AW // HD
    IH = w_uq_idx.shape[2] // HD
    BW = w_proj_b.shape[1]
    BH = BW // P
    DFF = w_mlp1.shape[2]
    TOPK = min(256, T // 4)
    RC, AC, MH = R // P, AW // P, DFF // P // 2
    assert (KC, TB, RC, AC, BH, IH, TOPK) == (8, 4, 2, 4, 4, 4, P) and 2 * HD == P and MH == 16

    C_QLAT = 0
    C_K = C_QLAT + R
    C_V = C_K + AW
    C_KIDX = C_V + AW
    C_WIDX = C_KIDX + HD
    C_B = C_WIDX + IH
    C_GA = C_B + 4 * BW
    C_GB = C_GA + D

    V_C, V_G1, V_G2, V_QG = 0, 8, 16, 24
    V_B1 = 26
    V_B2 = V_B1 + 2 * MH
    V_BADA = V_B2 + KC
    V_LB = V_BADA + 6 * KC
    V_OG = V_LB + 2 * BH
    V_HQ = V_OG + BH
    V_HK = V_HQ + 1
    assert V_HK == P - 1

    U_KIDX, U_WIDX, U_K, U_UQI, U_V, U_UQ, U_B = 2, 3, 4, 8, 9, 13, 14
    U_M = U_B + 16
    U_O = U_M + 3 * KC
    U_1 = [U_O + KC, U_O + KC + 2 * MH]
    U_2 = [u + MH for u in U_1]
    N_UNITS = U_2[1] + MH
    groups = [1] * N_UNITS
    groups[U_UQI], groups[U_UQ] = 2, 4
    for m in range(KC):
        groups[U_M + 3 * m + 2] = 2
    G = [0]
    for g in groups:
        G.append(G[-1] + g)

    E_O = G[U_M]
    E_1 = [E_O + KC, E_O + 2 * KC + MH]
    E_2 = [e + MH for e in E_1]

    T_U = 2 * KC + RC

    w_in_v = w_in[0].rearrange("(k p) n -> p k n", p=P)
    w_uq_v = w_uq[0].rearrange("(k p) (m n) -> p k m n", p=P, n=P)
    w_uqi_v = w_uq_idx[0].rearrange("(k p) (m n) -> p k m n", p=P, n=P)
    w_pa_v = w_proj_a[0].rearrange("(k p) n -> p k n", p=P)
    w_pb_v = w_proj_b[0].rearrange("(k p) n -> p k n", p=P)
    w_out_v = w_out[0].rearrange("(k p) n -> p k n", p=P)
    w_1_v = w_mlp1[0].rearrange("(k p) n -> p k n", p=P)
    w_2_v = w_mlp2[0].rearrange("(k p) n -> p k n", p=P)
    w_ada_v = w_ada[0].rearrange("(k p) (g n) -> g k p n", p=P, g=3)
    out_v = out[0].rearrange("(b p) (m n) -> m p b n", p=P, n=P)

    with ExitStack() as ctx:
        base = -(-nc.sbuf_base // 32) * 32
        KB = 1024
        at = {}

        def place(name, offset, shape, dt=F32):
            at[name] = nc.alloc_sbuf_tensor_at(name, shape, dt, offset=base + offset)
            return at[name]

        w_raw = place("w_raw", 0, [P, WS, 8, P])
        w_hi = place("w_hi", 16 * KB, [P, WS, 8, P], F32R)
        w_lo = place("w_lo", 32 * KB, [P, WS, 8, P], F32R)
        xT = place("xT", 48 * KB, [P, KC, T])
        h_hi = place("h_hi", 64 * KB, [P, KC, T], F32R)
        h_lo = place("h_lo", 80 * KB, [P, KC, T], F32R)
        RB = 96 * KB
        bT = place("bT", RB, [P, 4 * BH, T])
        ada_raw = place("ada_raw", RB, [P, 4, 2048])
        rt_k = place("rt_k", RB, [P, 4, T])
        vT = place("vT", RB + 16 * KB, [P, AC, T])
        ob_hi = place("ob_hi", RB, [P, BH, T], F32R)
        ob_lo = place("ob_lo", RB + 8 * KB, [P, BH, T], F32R)
        u_hi = place("u_hi", RB, [P, MH, T], F32R)
        RA = 128 * KB
        kT = place("kT", RA, [P, AC, T])
        qT = place("qT", RA + 8 * KB, [P, AC, T])
        score = place("score", RA + 16 * KB, [P, TB, T])
        v_nat = place("v_nat", RA + 24 * KB, [P, TB, T])
        i_nat = place("i_nat", RA + 32 * KB, [P, TB, T])
        ada_acc = place("ada_acc", RA, [P, 2048])
        x_nat = place("x_nat", RA + 24 * KB, [P, TB, D])
        oa_hi = place("oa_hi", RA + 8 * KB, [P, AC, T], F32R)
        oa_lo = place("oa_lo", RA, [P, AC, T], F32R)
        sig_a = place("sig_a", RA + 16 * KB, [P, 2, T])
        sig_b = place("sig_b", RA + 20 * KB, [P, 2, T])
        ada_acc2 = place("ada_acc2", RA + 24 * KB, [P, 2, 2048])
        u_lo = place("u_lo", RA, [P, MH, T], F32R)
        RL = 168 * KB
        latT = place("latT", RL, [P, RC, T])
        lat_hi = place("lat_hi", RL + 4 * KB, [P, RC, T], F32R)
        lat_lo = place("lat_lo", RL + 8 * KB, [P, RC, T], F32R)
        kiT = place("kiT", RL + 12 * KB, [P, T])
        wiT = place("wiT", RL + 14 * KB, [P, T])
        qiT = place("qiT", RL + 16 * KB, [P, RC, T])
        sq = place("sq", RL + 20 * KB, [P, 2, T])
        rt = place("rt", RL + 24 * KB, [P, 2, T])
        tmp = place("tmp", RL + 28 * KB, [P, 2, T])
        rel = place("rel", RL + 28 * KB, [P, 2, T])
        rt_q = place("rt_q", RL, [P, 4, T])
        pr = place("pr", RL, [P, 2, 1280])
        prT = place("prT", RL + 10 * KB, [P, 1280])
        hg_e = place("hg_e", RL + 15 * KB, [P, T])
        hg_k = place("hg_k", RL + 17 * KB, [P, T])
        hg_qk = place("hg_qk", RL + 19 * KB, [P, 2, T])
        hg_at = place("hg_at", RL + 23 * KB, [P, T])
        hg_kn = place("hg_kn", RL + 25 * KB, [P, T])
        hg_s = place("hg_s", RL + 27 * KB, [P, 3, P])
        hg_t = place("hg_t", RL + 29 * KB, [P, T])
        m_hi = place("m_hi", RL, [P, KC, T], F32R)
        m_lo = place("m_lo", RL + 16 * KB, [P, KC, T], F32R)
        sq_o = place("sq_o", RA + 16 * KB, [P, 2, T])
        rt_o = place("rt_o", RA + 20 * KB, [P, T])
        relu_u = place("relu_u", RL, [P, 2, T])
        sqr_u = place("sqr_u", RL + 4 * KB, [P, 2, T])
        o_stage = place("o_stage", RL + 8 * KB, [P, 2, TB, P])
        RC_ = 200 * KB
        ident = place("ident", RC_, [P, P])
        ones = place("ones", RC_ + 512, [P, P])
        twins = place("twins", RC_ + 1024, [P, P])
        causal = place("causal", RC_ + 1536, [P, P])
        col = place("col", RC_ + 2048, [P, P])
        vec = place("vec", RC_ + 2560, [P, P])
        mod = place("mod", RC_ + 3072, [P, 6 * KC])
        sc = place("sc", RC_ + 3072 + 192, [P, 64])
        wi_nat = place("wi_nat", RC_ + 3072 + 448, [P, TB, IH])
        top8 = place("top8", RC_ + 3072 + 512, [P, 3, 8])
        smx = place("smx", RC_ + 3072 + 608, [P, 3, AH, TB])
        lvl_mask = place("lvl_mask", RC_ + 3072 + 992, [P, 7, P], I8)
        A1, LBC, OML, CS, CA, KIG = (sc[:, 0:8], sc[:, 8:12], sc[:, 12:16], sc[:, 16:24], sc[:, 24:32],
                                     sc[:, 32:33])
        EPSC = sc[:, 33:34]
        LBD = sc[:, 34:38]
        A2 = sc[:, 40:48]
        SHIFT1, SCALE1, GATE1, SHIFT2, SCALE2, GATE2 = (mod[:, 8 * i:8 * i + 8] for i in range(6))

        bank = [ctx.enter_context(nc.psum_tensor(f"bank{i}", [P, T], F32)) for i in range(8)]

        def sem(name):
            return ctx.enter_context(nc.semaphore(name))

        vec_loaded, x_loaded = sem("vec_loaded"), sem("x_loaded")
        ada_loaded = [sem(f"ada_loaded{i}") for i in range(4)]
        w_loaded = [sem(f"w_loaded{i}") for i in range(WS)]
        hi_ready, lo_ready = sem("hi_ready"), sem("lo_ready")
        consts_ready, consts_step = sem("consts_ready"), sem("consts_step")
        dve_own, act_own = sem("dve_own"), sem("act_own")
        vec_turned, col_ready, lb_ready = sem("vec_turned"), sem("col_ready"), sem("lb_ready")
        x_turned, xT_ready = sem("x_turned"), sem("xT_ready")
        sq_ready, sq_summed, rt_ready, rt_used = (sem("sq_ready"), sem("sq_summed"), sem("rt_ready"),
                                                  sem("rt_used"))
        ada_used, mod_turned, mod_ready = sem("ada_used"), sem("mod_turned"), sem("mod_ready")
        t_ready, t_hi, t_lo = sem("t_ready"), sem("t_hi"), sem("t_lo")
        group_done, lin_evac = sem("group_done"), sem("lin_evac")
        wi_turned, wi_ready = sem("wi_turned"), sem("wi_ready")
        qk_normed = sem("qk_normed")
        score_done, rel_ready, rel_used = sem("score_done"), sem("rel_ready"), sem("rel_used")
        v_turned, v_ready = sem("v_turned"), sem("v_ready")
        i_turned, i_ready = sem("i_turned"), sem("i_ready")
        hg_sig, hg_gated = sem("hg_sig"), sem("hg_gated")
        lvl_ready, lvl_done, lvl_taken = sem("lvl_ready"), sem("lvl_done"), sem("lvl_taken")
        ks_ready, ks_turned, kn_ready, kv_done, s_ready, o_done = (
            sem("ks_ready"), sem("ks_turned"), sem("kn_ready"), sem("kv_done"), sem("s_ready"),
            sem("o_done"))
        osq_ready, osq_summed, ort_ready, o_ready, obhi_ready, ob_ready = (
            sem("osq_ready"), sem("osq_summed"), sem("ort_ready"), sem("o_ready"), sem("obhi_ready"),
            sem("ob_ready"))
        logit_done, logit_masked, nmax_ready, exp_done, prob_ready = (
            sem("logit_done"), sem("logit_masked"), sem("nmax_ready"), sem("exp_done"),
            sem("prob_ready"))
        prob_turned, probT_ready, pv_done, oahi_ready, oa_ready = (
            sem("prob_turned"), sem("probT_ready"), sem("pv_done"), sem("oahi_ready"), sem("oa_ready"))
        gates_ready = sem("gates_ready")
        merged_ready = sem("merged_ready")
        u_hi_ready = sem("u_hi_ready")
        y_turned, out_staged = sem("y_turned"), sem("out_staged")
        out_written = [sem("out_written0"), sem("out_written1")]

        block = ctx.enter_context(nc.Block())
        ds = bass.ds
        OFF_Q = [P * b * (b + 1) // 2 for b in range(TB)]
        OFF_K = [0, 512, 896, 1152]

        @block.sync
        def _(sp):
            for k in range(TB):
                sp.dma_start(x_nat[:, k], x[0, k * P:(k + 1) * P, :]).then_inc(x_loaded, 16)
            for k in range(KC):
                if k >= 4:
                    sp.wait_ge(ada_used, k - 3)
                sp.dma_start(ada_raw[:, k % 4], w_ada_v[0, k]).then_inc(ada_loaded[k % 4], 16)

            def load(n, slot, halves):
                if not isinstance(n, int) or n >= WS:
                    sp.wait_ge(lo_ready, n - WS + 1)
                for dst, src in halves:
                    sp.dma_start(dst, src).then_inc(w_loaded[slot], 16)

            def columns(view, slot, start, k0=0):
                return [(w_raw[:, slot, j:j + 4], view[:, k0 + j:k0 + j + 4, start]) for j in (0, 4)]

            load(0, 0, columns(w_in_v, 0, ds(C_QLAT, P)))
            load(1, 1, columns(w_in_v, 1, ds(C_QLAT + P, P)))
            load(2, 2, [(w_raw[:, 2, :, j * HD:(j + 1) * HD], w_in_v[:, :, C_KIDX:C_KIDX + HD])
                        for j in (0, 1)])
            load(3, 3, columns(w_in_v, 3, ds(C_WIDX, P)))
            for j in range(AC):
                n = U_K + j
                load(n, n % WS, columns(w_in_v, n % WS, ds(C_K + j * P, P)))
            s = U_UQI % WS
            load(U_UQI, s, [(w_raw[:, s, 4 * k:4 * k + 2], w_uqi_v[:, k]) for k in range(RC)])
            for j in range(AC):
                n = U_V + j
                load(n, n % WS, columns(w_in_v, n % WS, ds(C_V + j * P, P)))
            s = U_UQ % WS
            load(U_UQ, s, [(w_raw[:, s, 4 * k:4 * k + 4], w_uq_v[:, k]) for k in range(RC)])
            with sp.Fori(0, 4) as i:
                for j in range(4):
                    s = (U_B + j) % WS
                    load(4 * i + (U_B + j), s, columns(w_in_v, s, ds(((4 * i + j) * P + C_B), P)))
            with sp.Fori(0, 2) as i:
                for m in range(4):
                    for j, c0 in ((0, C_GA), (1, C_GB)):
                        s = (U_M + 3 * m + j) % WS
                        load(12 * i + (U_M + 3 * m + j), s, columns(w_in_v, s, ds(((4 * i + m) * P + c0), P)))
                    s = (U_M + 3 * m + 2) % WS
                    at_m = (4 * i + m) * P
                    sp.compute_val(at_m * 4)
                    load(12 * i + (U_M + 3 * m + 2), s,
                         [(w_raw[:, s, 0:4], w_pa_v[:, :, ds(at_m, P)]),
                          (w_raw[:, s, 4:8], w_pb_v[:, :, ds(at_m, P)])])
            with sp.Fori(0, 2) as i:
                for j in range(4):
                    s = (U_O + j) % WS
                    load(4 * i + (U_O + j), s, columns(w_out_v, s, ds(((4 * i + j) * P), P)))
            for half in range(2):
                with sp.Fori(0, 4) as i:
                    for j in range(4):
                        s = (U_1[half] + j) % WS
                        load(4 * i + (U_1[half] + j), s,
                             columns(w_1_v, s, ds(((4 * i + (MH * half + j)) * P), P)))
                with sp.Fori(0, 4) as i:
                    for j in range(4):
                        s = (U_2[half] + j) % WS
                        load(4 * i + (U_2[half] + j), s,
                             columns(w_2_v, s, ds(((2 * i + j // 2) * P), P), MH * half + 8 * (j % 2)))
            for m in range(KC):
                sp.wait_ge(out_staged, m + 1)
                sp.dma_start(out_v[m], o_stage[:, m % 2]).then_inc(out_written[m % 2], 16)
            for b in range(2):
                sp.wait_ge(out_written[b], 16 * KC // 2)

        @block.gpsimd
        def _(pool):
            steps = [0]

            def step(ins):
                steps[0] += 1
                ins.then_inc(consts_step, 1)
                pool.wait_ge(consts_step, steps[0])

            step(nc.gpsimd.memset(ident[:], 0.0))
            step(nc.gpsimd.affine_select(out=ident[:], in_=ident[:], compare_op=ALU.not_equal, fill=1.0,
                                         base=0, pattern=[[-1, P]], channel_multiplier=1))
            step(nc.gpsimd.memset(ones[:], 1.0))
            step(nc.gpsimd.memset(EPSC, EPS))
            step(nc.gpsimd.memset(twins[:], 0.0))
            step(nc.gpsimd.memset(twins[0:HD, 0:HD], 1.0))
            step(nc.gpsimd.memset(twins[HD:P, HD:P], 1.0))
            step(nc.gpsimd.memset(causal[:], 0.0))
            step(nc.gpsimd.affine_select(out=causal[:], in_=causal[:], compare_op=ALU.is_ge, fill=MASKED,
                                         base=0, pattern=[[-1, P]], channel_multiplier=1))
            step(nc.gpsimd.memset(lvl_mask[:], 0.0))
            for l in range(7):
                H = 1 << l
                second = lvl_mask[:, l].rearrange("p (b two h) -> p b two h", two=2, h=H)[:, :, 1, :]
                nb = P // (2 * H)
                step(nc.gpsimd.memset(second, 1.0))
                for cm, b0, st in ((1, 0, -2 * H), (-1, H - 1, 2 * H)):
                    last = nc.gpsimd.affine_select(out=second, in_=second, compare_op=ALU.is_ge, fill=0.0,
                                                   base=b0, pattern=[[st, nb], [0, H]],
                                                   channel_multiplier=cm)
                    if l < 6 or cm > 0:
                        step(last)
            last.then_inc(consts_ready, 1)

            def split_lo(n, s):
                pool.wait_ge(hi_ready, n + 1)
                nc.gpsimd.tensor_tensor(w_lo[:, s], w_raw[:, s], w_hi[:, s].bitcast(F32),
                                        ALU.subtract).then_inc(lo_ready, 1)

            with pool.Fori(0, N_UNITS // WS) as i:
                for s in range(WS):
                    split_lo(WS * i + s, s)
            for n in range(N_UNITS // WS * WS, N_UNITS):
                split_lo(n, n % WS)

        @block.scalar
        def _(act):
            own = [0]

            def step(ins):
                own[0] += 1
                ins.then_inc(act_own, 1)
                act.wait_ge(act_own, own[0])

            rows = [(V_C, c.rearrange("a (k n) -> (a k) n", n=P)),
                    (V_G1, norm1_g.rearrange("a (k n) -> (a k) n", n=P)),
                    (V_G2, norm2_g.rearrange("a (k n) -> (a k) n", n=P)),
                    (V_QG, q_lat_norm_g.rearrange("a (k n) -> (a k) n", n=P)),
                    (V_B1, b_mlp1.rearrange("a (k n) -> (a k) n", n=P)),
                    (V_B2, b_mlp2.rearrange("a (k n) -> (a k) n", n=P)),
                    (V_BADA, b_ada.rearrange("a (k n) -> (a k) n", n=P)),
                    (V_LB, hgrn_lb.rearrange("a (k n) -> (a k) n", n=P)),
                    (V_OG, hgrn_o_norm_g.rearrange("a (k n) -> (a k) n", n=P))]
            for r0, src in rows:
                act.dma_start(vec[r0:r0 + src.shape[0], :], src).then_inc(vec_loaded, 16)
            for r0, src in ((V_HQ, q_norm_g), (V_HK, k_norm_g)):
                for j in (0, HD):
                    act.dma_start(vec[r0:r0 + 1, j:j + HD], src).then_inc(vec_loaded, 16)
            for j in (0, HD):
                act.dma_start(sc[j:j + HD, 32:33], k_idx_norm_g.rearrange("a (n o) -> (a n) o", o=1),
                              allow_slow_non_contiguous=True).then_inc(vec_loaded, 16)

            def split_hi(n, s=None):
                if s is None:
                    s = n % WS
                    act.wait_ge(w_loaded[s], 32 * (n // WS + 1))
                nc.scalar.activation(w_hi[:, s], w_raw[:, s], ACT.Copy).then_inc(hi_ready, 1)

            def take(g, dst, b=None):
                act.wait_ge(group_done, g + 1)
                nc.scalar.activation(dst, bank[g % 2][:dst.shape[0]], ACT.Copy).then_inc(lin_evac, 1)

            act.wait_ge(vec_turned, 1)
            step(nc.scalar.activation(col[:], bank[0][:, 0:P], ACT.Copy))
            nc.scalar.activation(CS, col[:, V_C:V_C + KC], ACT.Sigmoid).then_inc(col_ready, 1)

            nsq = [0]

            def square(src, buf=sq):
                s = nsq[0]
                nsq[0] += 1
                if s >= 2:
                    act.wait_ge(sq_summed, s - 1)
                nc.scalar.activation(buf[:, s % 2], src, ACT.Square).then_inc(sq_ready, 1)

            for k in range(KC):
                act.wait_ge(x_turned, k + 1)
                square(bank[2 + k % 4][:])
                nc.scalar.activation(xT[:, k], bank[2 + k % 4][:], ACT.Copy).then_inc(xT_ready, 1)

            def root(j, s_last, dst, width):
                act.wait_ge(sq_summed, s_last + 1)
                nc.scalar.activation(dst, bank[6 + j % 2][:], ACT.Sqrt, scale=1.0 / width,
                                     bias=EPSC).then_inc(rt_ready, 1)

            act.wait_ge(consts_ready, 1)
            act.wait_ge(lb_ready, 1)
            nc.scalar.activation(LBC, LBC, ACT.Exp)
            nc.scalar.activation(OML, OML, ACT.Exp).then_inc(lb_ready, 1)
            root(0, 7, rt[:, 0], D)
            for n in range(WS):
                split_hi(n)
            act.wait_ge(mod_ready, 1)
            for k in range(KC):
                act.wait_ge(t_ready, k + 1)
                nc.scalar.activation(h_hi[:, k], tmp[:, k % 2], ACT.Identity,
                                     bias=SHIFT1[:, k:k + 1]).then_inc(t_hi, 1)

            take(0, latT[:, 0]); split_hi(4)
            take(1, latT[:, 1]); split_hi(5)
            act.wait_ge(lin_evac, 2)
            square(latT[:, 0]); square(latT[:, 1])
            take(2, kiT[:]); split_hi(6)
            act.wait_ge(lin_evac, 3)
            square(kiT[:])
            take(3, wiT[:]); split_hi(7)
            take(4, kT[:, 0]); split_hi(8)
            root(1, 9, rt[:, 1], R)
            for k in range(RC):
                act.wait_ge(t_ready, KC + k + 1)
                nc.scalar.activation(lat_hi[:, k], tmp[:, k % 2], ACT.Copy).then_inc(t_hi, 1)
            take(5, kT[:, 1]); split_hi(9)
            act.wait_ge(t_lo, KC)
            root(2, 10, rt[:, 0], HD)
            act.wait_ge(wi_turned, 1)
            nc.scalar.activation(wi_nat[:], bank[5][:, 0:TB * IH].rearrange("p (b h) -> p b h", b=TB),
                                 ACT.Copy).then_inc(wi_ready, 1)
            take(6, kT[:, 2]); split_hi(10)
            take(7, kT[:, 3]); split_hi(11)
            take(8, qiT[:, 0])
            take(9, qiT[:, 1]); split_hi(12)
            act.wait_ge(lin_evac, 8)
            for j in range(AC):
                square(kT[:, j])
                if j >= 1:
                    root(2 + j, 10 + j, rt_k[:, j - 1], HD)
            root(2 + AC, 10 + AC, rt_k[:, AC - 1], HD)

            nrel = [0]

            def relus(qb):
                n = (qb + 1) * P
                for h in range(IH):
                    s = nrel[0]
                    nrel[0] += 1
                    act.wait_ge(score_done, s + 1)
                    if s >= 2:
                        act.wait_ge(rel_used, s - 1)
                    nc.scalar.activation(rel[:, s % 2, 0:n], bank[2 + h][:, 0:n], ACT.Relu,
                                         scale=HD ** -0.5 * IH ** -0.5).then_inc(rel_ready, 1)

            take(10, vT[:, 0]); split_hi(13)
            relus(1)
            take(11, vT[:, 1]); split_hi(14)
            relus(2)
            take(12, vT[:, 2]); split_hi(15)
            relus(3)
            take(13, vT[:, 3]); split_hi(16)
            for j in range(AC):
                take(14 + j, qT[:, j])
            split_hi(17)
            for sb in range(TB):
                act.wait_ge(v_turned, sb + 1)
                nc.scalar.activation(v_nat[:, sb], bank[2 + sb][:], ACT.Copy).then_inc(v_ready, 1)

            act.wait_ge(rt_used, 1 + AC)

            def b_blocks(part):
                with act.Fori(0, 2) as i:
                    for j in range(4):
                        g = G[U_B] + 8 * part + j
                        act.wait_ge(group_done, 4 * i + (g + 1))
                        nc.scalar.activation(bT[:, ds(4 * i + (8 * part + j), 1)].rearrange("p o t -> p (o t)"),
                                             bank[g % 2][:], ACT.Copy).then_inc(lin_evac, 1)
                        n = U_B + 8 * part + j + WS
                        act.wait_ge(w_loaded[n % WS], 32 * i + 32 * (n // WS + 1))
                        split_hi(None, n % WS)

            b_blocks(0)
            for j in range(AC):
                square(qT[:, j])
                if j >= 1:
                    root(6 + j, 14 + j, rt_q[:, j - 1], HD)
            root(6 + AC, 14 + AC, rt_q[:, AC - 1], HD)
            b_blocks(1)

            act.wait_ge(lin_evac, G[U_M])
            for sb in range(TB):
                act.wait_ge(i_turned, sb + 1)
                nc.scalar.activation(i_nat[:, sb], bank[2 + sb][:], ACT.Copy).then_inc(i_ready, 1)
            act.wait_ge(rt_used, 1 + 2 * AC)
            for h in range(BH):
                if h >= 1:
                    act.wait_ge(obhi_ready, h)
                    act.wait_ge(ob_ready, h)
                nc.scalar.activation(hg_t[:], bT[:, h], ACT.Sigmoid).then_inc(hg_sig, 1)
                nc.scalar.activation(bT[:, BH + h], bT[:, BH + h], ACT.Sigmoid).then_inc(hg_sig, 1)
                act.wait_ge(hg_gated, 2 * h + 1)
                nc.scalar.activation(hg_t[:], bT[:, 3 * BH + h], ACT.Sigmoid).then_inc(hg_sig, 1)
                act.wait_ge(ks_turned, h + 1)
                nc.scalar.activation(hg_kn[:], bank[6][:], ACT.Copy).then_inc(kn_ready, 1)
                act.wait_ge(o_done, h + 1)
                nc.scalar.activation(hg_qk[:, 0], bank[5][:], ACT.Square).then_inc(osq_ready, 1)
                act.wait_ge(osq_summed, h + 1)
                nc.scalar.activation(hg_qk[:, 1], bank[7][:], ACT.Sqrt, scale=1.0 / P,
                                     bias=EPSC).then_inc(ort_ready, 1)
                act.wait_ge(o_ready, h + 1)
                nc.scalar.activation(ob_hi[:, h], hg_t[:], ACT.Copy).then_inc(obhi_ready, 1)

            for h in range(AH + 1):
                if h < AH:
                    for qb in range(TB):
                        n = (qb + 1) * P
                        if qb == 0:
                            act.wait_ge(nmax_ready, h + 1)
                        p = pr[:, h % 2, OFF_Q[qb]:OFF_Q[qb] + n]
                        nc.scalar.activation(p, p, ACT.Exp, scale=HD ** -0.5,
                                             bias=smx[:, 1, h, qb:qb + 1],
                                             accum_out=smx[:, 2, h, qb:qb + 1]).then_inc(exp_done, 1)
                if h >= 1:
                    for kb in range(TB):
                        act.wait_ge(prob_turned, TB * (h - 1) + kb + 1)
                        if h >= 2 and kb == 0:
                            act.wait_ge(pv_done, h - 1)
                        w = T - kb * P
                        nc.scalar.activation(prT[:, OFF_K[kb]:OFF_K[kb] + w], bank[2 + kb][:, kb * P:T],
                                             ACT.Copy).then_inc(probT_ready, 1)
                    if (h - 1) % 2 == 1:
                        j = (h - 1) // 2
                        act.wait_ge(pv_done, h)
                        nc.scalar.activation(oa_hi[:, j], bank[j % 2][:], ACT.Copy).then_inc(oahi_ready, 1)

            act.wait_ge(ob_ready, BH)
            with act.Fori(0, 2) as i:
                for m in range(4):
                    for j in range(2):
                        src = w_ada_v[ds(i + 1, 1), 2 * m + j].rearrange("o p n -> p (o n)")
                        act.wait_ge(ada_used, 8 * i + (8 + 2 * m + j - 1))
                        act.dma_start(ada_raw[:, 2 + j], src).then_inc(ada_loaded[2 + j], 16)
                    for j in range(3):
                        n = U_M + 3 * m + j
                        act.wait_ge(group_done, 16 * i + G[n + 1])
                        if j < 2:
                            if j == 0:
                                act.wait_ge(merged_ready, 4 * i + (m + 1))
                            dst = (sig_a, sig_b)[j]
                            nc.scalar.activation(dst[:, m % 2], bank[4 * (m % 2) + j][:],
                                                 ACT.Sigmoid).then_inc(gates_ready, 1)
                        n4 = n + WS
                        act.wait_ge(w_loaded[n4 % WS], 96 * i + 32 * (n4 // WS + 1))
                        split_hi(None, n4 % WS)

            for m in range(KC):
                act.wait_ge(lin_evac, E_O + m + 1)
                square(xT[:, m], sq_o)
                split_hi(U_O + m + WS)
            root(11, 26, rt_o[:], D)
            for k in range(KC):
                act.wait_ge(t_ready, KC + RC + k + 1)
                nc.scalar.activation(h_hi[:, k], tmp[:, k % 2], ACT.Identity,
                                     bias=SHIFT2[:, k:k + 1]).then_inc(t_hi, 1)

            for half in range(2):
                with act.Fori(0, 4) as i:
                    for j in range(4):
                        n = U_1[half] + j
                        act.wait_ge(group_done, 4 * i + G[n + 1])
                        act.wait_ge(t_lo, 4 * i + (T_U + MH * half + j - 1))
                        nc.scalar.activation(relu_u[:, j % 2], bank[G[n] % 2][:], ACT.Relu,
                                             bias=col[:, ds(4 * i + (V_B1 + MH * half + j), 1)]
                                             ).then_inc(lin_evac, 1)
                        act.wait_ge(lin_evac, 4 * i + (E_1[half] + j + 1))
                        nc.scalar.activation(u_hi[:, ds(4 * i + j, 1)].rearrange("p o t -> p (o t)"),
                                             relu_u[:, j % 2], ACT.Square).then_inc(u_hi_ready, 1)
                        act.wait_ge(w_loaded[n % WS], 32 * i + 32 * (n // WS + 2))
                        split_hi(None, n % WS)
                with act.Fori(0, 3 if half else 4) as i:
                    for j in range(4):
                        n = U_2[half] + j
                        act.wait_ge(group_done, 4 * i + G[n + 1])
                        act.wait_ge(w_loaded[n % WS], 32 * i + 32 * (n // WS + 2))
                        split_hi(None, n % WS)

            for m in range(KC):
                act.wait_ge(y_turned, m + 1)
                if m >= 2:
                    act.wait_ge(out_written[m % 2], 16 * (m // 2))
                nc.scalar.activation(o_stage[:, m % 2], bank[2 + m % 2][:].rearrange("p (b n) -> p b n", b=TB),
                                     ACT.Copy).then_inc(out_staged, 1)

        @block.vector
        def _(dve):
            own = [0]

            def step(ins):
                own[0] += 1
                ins.then_inc(dve_own, 1)
                dve.wait_ge(dve_own, own[0])

            v = nc.vector
            dve.wait_ge(consts_ready, 1)
            dve.wait_ge(col_ready, 1)
            step(v.tensor_tensor(CA, CS, col[:, V_C:V_C + KC], ALU.mult))
            dve.wait_ge(vec_loaded, 16 * 15)
            step(v.tensor_tensor(LBD, col[:, V_LB:V_LB + BH], col[:, V_LB + BH:V_LB + 2 * BH], ALU.max))
            v.tensor_tensor(LBC, col[:, V_LB:V_LB + BH], LBD, ALU.subtract)
            v.tensor_tensor(OML, col[:, V_LB + BH:V_LB + 2 * BH], LBD, ALU.subtract).then_inc(lb_ready, 1)

            def ada_sum(acc, k, slot, loaded):
                dve.wait_ge(ada_loaded[slot], loaded)
                if k == 0:
                    v.tensor_scalar(acc, ada_raw[:, slot], CA[:, 0:1], None, ALU.mult).then_inc(ada_used, 1)
                else:
                    v.scalar_tensor_tensor(out=acc, in0=ada_raw[:, slot], scalar=CA[:, k:k + 1], in1=acc,
                                           op0=ALU.mult, op1=ALU.add).then_inc(ada_used, 1)

            for k in range(KC):
                if k >= 1:
                    dve.wait_ge(ada_used, k)
                ada_sum(ada_acc[:], k, k % 4, 16 * (k // 4 + 1))
                if k == 3:
                    dve.wait_ge(rt_ready, 1)
                    step(v.reciprocal(rt[:, 0], rt[:, 0]))
            dve.wait_ge(mod_turned, 1)
            step(v.tensor_tensor(mod[:, 0:2 * KC], bank[1][:, 0:2 * KC], col[:, V_BADA:V_BADA + 2 * KC],
                                 ALU.add))
            v.scalar_tensor_tensor(out=A1, in0=SCALE1, scalar=1.0, in1=col[:, V_G1:V_G1 + KC], op0=ALU.add,
                                   op1=ALU.mult).then_inc(mod_ready, 1)
            dve.wait_ge(mod_ready, 1)

            nt = [0]

            def scaled(src, g, rr):
                s = nt[0]
                nt[0] += 1
                if s >= 2:
                    dve.wait_ge(t_lo, s - 1)
                v.scalar_tensor_tensor(out=tmp[:, s % 2], in0=src, scalar=g, in1=rr, op0=ALU.mult,
                                       op1=ALU.mult).then_inc(t_ready, 1)
                return s

            def lows(s, shift, hi, lo):
                dve.wait_ge(t_hi, s + 1)
                if shift is None:
                    v.tensor_tensor(lo, tmp[:, s % 2], hi.bitcast(F32), ALU.subtract).then_inc(t_lo, 1)
                else:
                    v.scalar_tensor_tensor(out=lo, in0=tmp[:, s % 2], scalar=shift, in1=hi.bitcast(F32),
                                           op0=ALU.add, op1=ALU.subtract).then_inc(t_lo, 1)

            def norm_split(src, gains, rr, shifts, hi, lo, n):
                prev = None
                for k in range(n + 1):
                    if k < n:
                        s = scaled(src[:, k], gains[:, k:k + 1], rr)
                    if prev is not None:
                        kk = k - 1
                        lows(prev, None if shifts is None else shifts[:, kk:kk + 1], hi[:, kk], lo[:, kk])
                    prev = s

            norm_split(xT, A1, rt[:, 0], SHIFT1, h_hi, h_lo, KC)
            dve.wait_ge(rt_ready, 2)
            step(v.reciprocal(rt[:, 1], rt[:, 1]))
            norm_split(latT, col[:, V_QG:V_QG + RC], rt[:, 1], None, lat_hi, lat_lo, RC)

            def head_norm(j, dst, g, rr):
                dve.wait_ge(rt_ready, j + 1)
                step(v.reciprocal(rr, rr))
                v.scalar_tensor_tensor(out=dst, in0=dst, scalar=g, in1=rr, op0=ALU.mult,
                                       op1=ALU.mult).then_inc(rt_used, 1)

            head_norm(2, kiT[:], KIG, rt[:, 0])
            for j in range(AC):
                head_norm(3 + j, kT[:, j], col[:, V_HK:V_HK + 1], rt_k[:, j])

            dve.wait_ge(wi_ready, 1)
            s = 0
            for qb in range(1, TB):
                n = (qb + 1) * P
                for h in range(IH):
                    dve.wait_ge(rel_ready, s + 1)
                    w = wi_nat[:, qb, h:h + 1]
                    if h == 0:
                        v.tensor_scalar(score[:, qb, 0:n], rel[:, s % 2, 0:n], w, None,
                                        ALU.mult).then_inc(rel_used, 1)
                    else:
                        dve.wait_ge(rel_used, s)
                        v.scalar_tensor_tensor(out=score[:, qb, 0:n], in0=rel[:, s % 2, 0:n], scalar=w,
                                               in1=score[:, qb, 0:n], op0=ALU.mult,
                                               op1=ALU.add).then_inc(rel_used, 1)
                    s += 1
                dve.wait_ge(rel_used, s)
                diag = score[:, qb, qb * P:n]
                step(v.tensor_tensor(diag, diag, causal[:], ALU.add))
            base_own = own[0]
            assert base_own >= 2
            for i in range(TOPK // 8):
                for r in range(2):
                    for qb in range(1, TB):
                        n = (qb + 1) * P
                        dve.wait_ge(dve_own, base_own + 6 * i + 3 * r + qb - 3)
                        if r == 0:
                            v.max(top8[:, qb - 1], score[:, qb, 0:n]).then_inc(dve_own, 1)
                        else:
                            v.match_replace(score[:, qb, 0:n], top8[:, qb - 1], score[:, qb, 0:n],
                                            TAKEN).then_inc(dve_own, 1)
            own[0] += 6 * (TOPK // 8)
            dve.wait_ge(dve_own, own[0])
            for qb in range(1, TB):
                n = (qb + 1) * P
                v.tensor_scalar(score[:, qb, 0:n], score[:, qb, 0:n], TAKEN_BELOW, FORBID, ALU.is_gt,
                                ALU.mult)
            step(v.tensor_scalar(score[:, 0, 0:P], causal[:], 0.0, FORBID, ALU.is_lt, ALU.mult))

            for j in range(AC):
                head_norm(7 + j, qT[:, j], col[:, V_HQ:V_HQ + 1], rt_q[:, j])

            dve.wait_ge(rt_used, 1 + 2 * AC)

            nl = [0]
            for h in range(BH):
                q, f, g = bT[:, h], bT[:, BH + h], bT[:, 3 * BH + h]
                if h == 0:
                    dve.wait_ge(lb_ready, 2)
                    step(v.tensor_tensor(LBD, LBC, OML, ALU.add))
                    step(v.reciprocal(LBD, LBD))
                    v.tensor_tensor(LBC, LBC, LBD, ALU.mult)
                    step(v.tensor_tensor(OML, OML, LBD, ALU.mult))
                dve.wait_ge(hg_sig, 3 * h + 1)
                v.tensor_tensor(q, q, hg_t[:], ALU.mult).then_inc(hg_gated, 1)
                dve.wait_ge(hg_sig, 3 * h + 2)
                step(v.tensor_scalar(f, f, OML[:, h:h + 1], LBC[:, h:h + 1], ALU.mult, ALU.add))
                v.tensor_scalar(hg_k[:], f, -1.0, 1.0, ALU.mult, ALU.add).then_inc(lvl_ready, 1)
                dve.wait_ge(lvl_ready, 8 * h + 1)
                step(v.memset(hg_e[:], 1.0))
                dve.wait_ge(hg_sig, 3 * h + 3)
                v.tensor_tensor(g, g, hg_t[:], ALU.mult).then_inc(hg_gated, 1)
                dve.wait_ge(hg_gated, 2 * h + 2)

                def taken(l):
                    dve.wait_ge(lvl_done, 8 * h + l + 2)
                    src = bank[2 + (l + 1) % 2][:].rearrange("p (b t) -> p b t", b=TB)
                    dst = hg_at[:].rearrange("p (b t) -> p b t", b=TB)
                    if l < 0:
                        v.tensor_tensor(dst, src, ident[:].unsqueeze(1).to_broadcast([P, TB, P]),
                                        ALU.mult).then_inc(lvl_taken, 1)
                    else:
                        dve.wait_ge(lvl_taken, 8 * h + l + 1)
                        v.copy_predicated(dst, lvl_mask[:, l].unsqueeze(1).to_broadcast([P, TB, P]),
                                          src).then_inc(lvl_taken, 1)

                for l in range(7):
                    H = 1 << l

                    def halves(t):
                        w = t.rearrange("p (b two h) -> p b two h", two=2, h=H)
                        return w[:, :, 0, :], w[:, :, 1, :]

                    (k1, _), (_, q2), (e1, _), (f1, f2) = (halves(hg_k[:]), halves(q), halves(hg_e[:]),
                                                           halves(f))
                    d1, d2 = halves(hg_qk[:, l % 2])
                    shape = [P, T // (2 * H), H]
                    if l >= 2:
                        dve.wait_ge(lvl_done, 8 * h + l)
                    v.tensor_tensor(d2, q2, f2, ALU.mult)
                    v.tensor_tensor(d1, k1, e1, ALU.mult).then_inc(lvl_ready, 1)
                    step(v.tensor_tensor(e1, e1, f2[:, :, H - 1:H].to_broadcast(shape), ALU.mult))
                    step(v.tensor_tensor(f2, f2, f1[:, :, H - 1:H].to_broadcast(shape), ALU.mult))
                    taken(l - 1)
                taken(6)
                dve.wait_ge(lvl_done, 8 * h + 8)
                v.tensor_tensor(hg_k[:], hg_k[:], hg_e[:], ALU.mult).then_inc(ks_ready, 1)
                step(v.tensor_tensor(q, q, f, ALU.mult))
                for b in range(TB - 1):
                    dve.wait_ge(kv_done, (TB - 1) * (h + 1))
                    kv = bank[4][:, b * P:(b + 1) * P]
                    if b == 0:
                        v.tensor_copy(hg_s[:, 0], kv).then_inc(s_ready, 1)
                    else:
                        dve.wait_ge(s_ready, (TB - 1) * h + b)
                        v.scalar_tensor_tensor(out=hg_s[:, b], in0=hg_s[:, b - 1],
                                               scalar=f[:, (b + 1) * P - 1:(b + 1) * P], in1=kv,
                                               op0=ALU.mult, op1=ALU.add).then_inc(s_ready, 1)
                dve.wait_ge(ort_ready, h + 1)
                step(v.reciprocal(hg_qk[:, 1], hg_qk[:, 1]))
                step(v.scalar_tensor_tensor(out=hg_t[:], in0=bank[5][:], scalar=col[:, V_OG + h:V_OG + h + 1],
                                            in1=hg_qk[:, 1], op0=ALU.mult, op1=ALU.mult))
                v.tensor_tensor(hg_t[:], hg_t[:], g, ALU.mult).then_inc(o_ready, 1)
                dve.wait_ge(obhi_ready, h + 1)
                v.tensor_tensor(ob_lo[:, h], hg_t[:], ob_hi[:, h].bitcast(F32),
                                ALU.subtract).then_inc(ob_ready, 1)

            for h in range(AH + 1):
                if h < AH:
                    for qb in range(TB):
                        i = TB * h + qb
                        n = (qb + 1) * P
                        dve.wait_ge(logit_done, i + 1)
                        if h >= 2 and qb == 0:
                            dve.wait_ge(prob_turned, TB * (h - 1))
                        v.tensor_tensor_reduce(
                            out=pr[:, h % 2, OFF_Q[qb]:OFF_Q[qb] + n], in0=bank[6 + i % 2][:, 0:n],
                            in1=score[:, qb, 0:n], scale=1.0, scalar=TAKEN, op0=ALU.add, op1=ALU.max,
                            accum_out=smx[:, 0, h, qb:qb + 1]).then_inc(logit_masked, 1)
                    dve.wait_ge(logit_masked, TB * (h + 1))
                    v.tensor_scalar(smx[:, 1, h], smx[:, 0, h], -(HD ** -0.5), None,
                                    ALU.mult).then_inc(nmax_ready, 1)
                if h >= 2 and h % 2 == 0:
                    j = h // 2 - 1
                    dve.wait_ge(oahi_ready, j + 1)
                    v.tensor_tensor(oa_lo[:, j], bank[j % 2][:], oa_hi[:, j].bitcast(F32),
                                    ALU.subtract).then_inc(oa_ready if j < 2 else merged_ready, 1)
                if h < AH:
                    dve.wait_ge(exp_done, TB * (h + 1))
                    step(v.reciprocal(smx[:, 2, h], smx[:, 2, h]))
                    for qb in range(TB):
                        p = pr[:, h % 2, OFF_Q[qb]:OFF_Q[qb] + (qb + 1) * P]
                        v.tensor_scalar(p, p, smx[:, 2, h, qb:qb + 1], None,
                                        ALU.mult).then_inc(prob_ready, 1)

            with dve.Fori(0, 2) as i:
                for m in range(4):
                    for j in range(2):
                        k = 2 * m + j
                        dve.wait_ge(ada_loaded[2 + j], 64 * i + (32 + 16 * (m + 1)))
                        dve.wait_ge(ada_used, 8 * i + (8 + k))
                        acc = ada_acc2[:, ds(i, 1)].rearrange("p o n -> p (o n)")
                        if k == 0:
                            v.tensor_scalar(acc, ada_raw[:, 2 + j], CA[:, 0:1], None,
                                            ALU.mult).then_inc(ada_used, 1)
                        else:
                            v.scalar_tensor_tensor(out=acc, in0=ada_raw[:, 2 + j], scalar=CA[:, k:k + 1],
                                                   in1=acc, op0=ALU.mult, op1=ALU.add).then_inc(ada_used, 1)
                    dve.wait_ge(gates_ready, 8 * i + (2 * m + 2))
                    dve.wait_ge(group_done, 16 * i + G[U_M + 3 * m + 3])
                    b = 4 * (m % 2)
                    own0 = own[0] + 4 * m
                    v.tensor_tensor(sig_a[:, m % 2], bank[b + 2][:], sig_a[:, m % 2],
                                    ALU.mult).then_inc(dve_own, 1)
                    v.tensor_tensor(sig_b[:, m % 2], bank[b + 3][:], sig_b[:, m % 2],
                                    ALU.mult).then_inc(dve_own, 1)
                    dve.wait_ge(dve_own, 16 * i + (own0 + 2))
                    v.tensor_tensor(sig_a[:, m % 2], sig_a[:, m % 2], sig_b[:, m % 2],
                                    ALU.add).then_inc(dve_own, 1)
                    dve.wait_ge(dve_own, 16 * i + (own0 + 3))
                    mh = m_hi[:, ds(4 * i + m, 1)].rearrange("p o t -> p (o t)")
                    ml = m_lo[:, ds(4 * i + m, 1)].rearrange("p o t -> p (o t)")
                    v.tensor_copy(mh, sig_a[:, m % 2]).then_inc(dve_own, 1)
                    dve.wait_ge(dve_own, 16 * i + (own0 + 4))
                    v.tensor_tensor(ml, sig_a[:, m % 2], mh.bitcast(F32),
                                    ALU.subtract).then_inc(merged_ready, 1)
            own[0] += 32
            dve.wait_ge(ada_used, 24)
            dve.wait_ge(mod_turned, 2)
            step(v.tensor_tensor(mod[:, 2 * KC:], bank[2][:, 0:4 * KC], col[:, V_BADA + 2 * KC:V_BADA + 6 * KC],
                                 ALU.add))
            v.scalar_tensor_tensor(out=A2, in0=SCALE2, scalar=1.0, in1=col[:, V_G2:V_G2 + KC], op0=ALU.add,
                                   op1=ALU.mult).then_inc(mod_ready, 1)
            dve.wait_ge(mod_ready, 2)
            for m in range(KC):
                g = G[U_O + m]
                dve.wait_ge(group_done, g + 1)
                v.scalar_tensor_tensor(out=xT[:, m], in0=bank[g % 2][:], scalar=GATE1[:, m:m + 1],
                                       in1=xT[:, m], op0=ALU.mult, op1=ALU.add).then_inc(lin_evac, 1)
            dve.wait_ge(rt_ready, 12)
            step(v.reciprocal(rt_o[:], rt_o[:]))
            norm_split(xT, A2, rt_o[:], SHIFT2, h_hi, h_lo, KC)
            dve.wait_ge(t_lo, 2 * KC + RC)

            for half in range(2):
                with dve.Fori(0, 4) as i:
                    for j in range(4):
                        own0 = own[0] + j
                        dve.wait_ge(lin_evac, 4 * i + (E_1[half] + j + 1))
                        v.tensor_tensor(sqr_u[:, j % 2], relu_u[:, j % 2], relu_u[:, j % 2],
                                        ALU.mult).then_inc(dve_own, 1)
                        dve.wait_ge(dve_own, 4 * i + (own0 + 1))
                        dve.wait_ge(u_hi_ready, 4 * i + (16 * half + j + 1))
                        v.tensor_tensor(u_lo[:, ds(4 * i + j, 1)].rearrange("p o t -> p (o t)"),
                                        sqr_u[:, j % 2],
                                        u_hi[:, ds(4 * i + j, 1)].rearrange("p o t -> p (o t)").bitcast(F32),
                                        ALU.subtract).then_inc(t_lo, 1)
                own[0] += 16
                for m in range(KC):
                    dve.wait_ge(group_done, G[U_2[half]] + 2 * m + 2)
                    if half == 0:
                        step(v.tensor_scalar(sqr_u[:, m % 2], bank[m % 2][:],
                                             col[:, V_B2 + m:V_B2 + m + 1], GATE2[:, m:m + 1], ALU.add,
                                             ALU.mult))
                        v.tensor_tensor(xT[:, m], xT[:, m], sqr_u[:, m % 2], ALU.add).then_inc(lin_evac, 1)
                    else:
                        dve.wait_ge(lin_evac, E_2[0] + KC)
                        v.scalar_tensor_tensor(out=xT[:, m], in0=bank[m % 2][:], scalar=GATE2[:, m:m + 1],
                                               in1=xT[:, m], op0=ALU.mult, op1=ALU.add).then_inc(lin_evac, 1)

        @block.tensor
        def _(pe):
            mm = nc.tensor.matmul

            def product(slot, b, rhs_hi, rhs_lo, js, first=True, last=True, before=None):
                n = len(js)
                for i, j in enumerate(js):
                    if before:
                        before(i)
                    f, l = first and i == 0, last and i == n - 1
                    mm(bank[b][:], w_hi[:, slot, j], rhs_hi(i), start=f, stop=False)
                    mm(bank[b][:], w_hi[:, slot, j], rhs_lo(i), start=False, stop=False)
                    end = mm(bank[b][:], w_lo[:, slot, j], rhs_hi(i), start=False, stop=l)
                end.then_inc(group_done, 1)

            def h_rhs(t):
                return lambda k: t[:, k]

            def unit(n, before=None):
                g = G[n]
                pe.wait_ge(lo_ready, n + 1)
                if g >= 2:
                    pe.wait_ge(lin_evac, g - 1)
                product(n % WS, g % 2, h_rhs(h_hi), h_rhs(h_lo), range(KC), before=before)

            pe.wait_ge(consts_ready, 1)
            pe.wait_ge(vec_loaded, 16 * 15)
            nc.tensor.transpose(bank[0][:, 0:P], vec[:], ident[:]).then_inc(vec_turned, 1)
            ns = [0]

            def sum_square(j, first, last, ones_, buf=sq):
                s = ns[0]
                ns[0] += 1
                pe.wait_ge(sq_ready, s + 1)
                if first and j >= 2:
                    pe.wait_ge(rt_ready, j - 1)
                mm(bank[6 + j % 2][:], ones_[:], buf[:, s % 2], start=first, stop=last
                   ).then_inc(sq_summed, 1)

            def sum_squares(j, n, ones_):
                for i in range(n):
                    sum_square(j, i == 0, i == n - 1, ones_)

            pe.wait_ge(x_loaded, 16 * TB)
            for k in range(KC):
                if k >= 4:
                    pe.wait_ge(xT_ready, k - 3)
                for b in range(TB):
                    end = nc.tensor.transpose(bank[2 + k % 4][:, b * P:(b + 1) * P],
                                              x_nat[:, b, k * P:(k + 1) * P], ident[:])
                end.then_inc(x_turned, 1)
                if k:
                    sum_square(0, k == 1, False, ones)
            sum_square(0, False, True, ones)
            pe.wait_ge(ada_used, KC)
            for j in range(2 * KC):
                end = mm(bank[1][:, j:j + 1], ada_acc[:, j * P:(j + 1) * P], ones[:, 0:1], start=True,
                         stop=True)
            end.then_inc(mod_turned, 1)
            pe.wait_ge(mod_ready, 1)
            unit(0, before=lambda k: pe.wait_ge(t_lo, k + 1))
            for n in (1, 2, 3, 4):
                unit(n)
            sum_squares(1, RC, ones)
            unit(5)
            sum_squares(2, 1, twins)
            for b in range(TB):
                end = nc.tensor.transpose(bank[5][:, b * IH:(b + 1) * IH], wiT[0:IH, b * P:(b + 1) * P],
                                          ident[0:IH, 0:IH])
            end.then_inc(wi_turned, 1)
            unit(6)
            unit(7)
            pe.wait_ge(lo_ready, U_UQI + 1)
            pe.wait_ge(t_lo, KC + RC)
            for m in range(2):
                g = G[U_UQI] + m
                pe.wait_ge(lin_evac, g - 1)
                product(U_UQI % WS, g % 2, h_rhs(lat_hi), h_rhs(lat_lo), [4 * k + m for k in range(RC)])
            for j in range(AC):
                sum_squares(3 + j, 1, twins)
            nscore = [0]

            def scores(qb):
                n = (qb + 1) * P
                for h in range(IH):
                    r = HD * (h % 2)
                    s = nscore[0]
                    nscore[0] += 1
                    if s >= IH:
                        pe.wait_ge(rel_ready, s - IH + 1)
                    mm(bank[2 + h][:, 0:n], qiT[r:r + HD, h // 2, qb * P:(qb + 1) * P], kiT[r:r + HD, 0:n],
                       start=True, stop=True).then_inc(score_done, 1)

            unit(9)
            pe.wait_ge(lin_evac, 10)
            pe.wait_ge(rt_used, 1)
            pe.wait_ge(wi_ready, 1)
            scores(1)
            unit(10)
            scores(2)
            unit(11)
            scores(3)
            unit(12)
            pe.wait_ge(lo_ready, U_UQ + 1)
            for m in range(AC):
                g = G[U_UQ] + m
                pe.wait_ge(lin_evac, g - 1)
                product(U_UQ % WS, g % 2, h_rhs(lat_hi), h_rhs(lat_lo), [4 * k + m for k in range(RC)])
            pe.wait_ge(rel_ready, 3 * IH)
            for sb in range(TB):
                for j in range(AC):
                    end = nc.tensor.transpose(bank[2 + sb][:, j * P:(j + 1) * P], vT[:, j, sb * P:(sb + 1) * P],
                                              ident[:])
                end.then_inc(v_turned, 1)

            def b_blocks(part):
                with pe.Fori(0, 2) as i:
                    for j in range(4):
                        n = U_B + 8 * part + j
                        g = G[n]
                        pe.wait_ge(lo_ready, 4 * i + (n + 1))
                        pe.wait_ge(lin_evac, 4 * i + (g - 1))
                        product(n % WS, g % 2, h_rhs(h_hi), h_rhs(h_lo), range(KC))

            b_blocks(0)
            for j in range(AC):
                sum_squares(7 + j, 1, twins)
            b_blocks(1)

            pe.wait_ge(lin_evac, G[U_M])
            pe.wait_ge(v_ready, TB)
            pe.wait_ge(rt_ready, 11)
            for sb in range(TB):
                for j in range(BH):
                    end = nc.tensor.transpose(bank[2 + sb][:, j * P:(j + 1) * P],
                                              bT[:, 2 * BH + j, sb * P:(sb + 1) * P], ident[:])
                end.then_inc(i_turned, 1)
            pe.wait_ge(i_ready, TB)
            for h in range(BH):
                q = bT[:, h]
                for l in range(-1, 7):
                    if l < 0:
                        pe.wait_ge(hg_gated, 2 * h + 1)
                    pe.wait_ge(lvl_ready, 8 * h + l + 2)
                    if h or l >= 1:
                        pe.wait_ge(lvl_taken, 8 * h + l)
                    for b in range(TB):
                        t = slice(b * P, (b + 1) * P)
                        lhs, rhs = (hg_k[:, t], q[:, t]) if l < 0 else (hg_qk[:, l % 2, t], hg_qk[:, l % 2, t])
                        end = mm(bank[2 + (l + 1) % 2][:, t], lhs, rhs, start=True, stop=True)
                    end.then_inc(lvl_done, 1)
                pe.wait_ge(ks_ready, h + 1)
                if h:
                    pe.wait_ge(kn_ready, h)
                for b in range(TB):
                    t = slice(b * P, (b + 1) * P)
                    end = nc.tensor.transpose(bank[6][:, t], hg_k[:, t], ident[:])
                end.then_inc(ks_turned, 1)
                pe.wait_ge(kn_ready, h + 1)
                if h:
                    pe.wait_ge(s_ready, (TB - 1) * h)
                for b in range(TB - 1):
                    t = slice(b * P, (b + 1) * P)
                    mm(bank[4][:, t], hg_kn[:, t], i_nat[:, b, h * P:(h + 1) * P], start=True,
                       stop=True).then_inc(kv_done, 1)
                pe.wait_ge(lvl_taken, 8 * h + 8)
                pe.wait_ge(s_ready, (TB - 1) * (h + 1))
                if h:
                    pe.wait_ge(o_ready, h)
                for b in range(TB):
                    t = slice(b * P, (b + 1) * P)
                    end = mm(bank[5][:, t], i_nat[:, b, h * P:(h + 1) * P], hg_at[:, t], start=True,
                             stop=b == 0)
                    if b:
                        end = mm(bank[5][:, t], hg_s[:, b - 1], q[:, t], start=False, stop=True)
                end.then_inc(o_done, 1)
                pe.wait_ge(osq_ready, h + 1)
                if h:
                    pe.wait_ge(ort_ready, h)
                mm(bank[7][:], ones[:], hg_qk[:, 0], start=True, stop=True).then_inc(osq_summed, 1)

            pe.wait_ge(ob_ready, BH)
            pe.wait_ge(rt_used, 1 + 2 * AC)
            for h in range(AH + 1):
                if h < AH:
                    r = HD * (h % 2)
                    for qb in range(TB):
                        i = TB * h + qb
                        n = (qb + 1) * P
                        if i >= 2:
                            pe.wait_ge(logit_masked, i - 1)
                        mm(bank[6 + i % 2][:, 0:n], qT[r:r + HD, h // 2, qb * P:(qb + 1) * P],
                           kT[r:r + HD, h // 2, 0:n], start=True, stop=True).then_inc(logit_done, 1)
                if h >= 1:
                    g = h - 1
                    r = HD * (g % 2)
                    j = g // 2
                    for kb in range(TB):
                        if g:
                            pe.wait_ge(probT_ready, TB * (g - 1) + kb + 1)
                        for qb in range(kb, TB):
                            pe.wait_ge(prob_ready, TB * g + qb + 1)
                            o = OFF_Q[qb] + kb * P
                            end = nc.tensor.transpose(bank[2 + kb][:, qb * P:(qb + 1) * P],
                                                      pr[:, g % 2, o:o + P], ident[:])
                        end.then_inc(prob_turned, 1)
                    if j >= 2:
                        pe.wait_ge(oa_ready, j - 1)
                    for kb in range(TB):
                        pe.wait_ge(probT_ready, TB * g + kb + 1)
                        w = T - kb * P
                        end = mm(bank[j % 2][r:r + HD, kb * P:T], v_nat[:, kb, g * HD:(g + 1) * HD],
                                 prT[:, OFF_K[kb]:OFF_K[kb] + w], start=kb == 0, stop=kb == TB - 1)
                    end.then_inc(pv_done, 1)

            pe.wait_ge(merged_ready, 2)
            with pe.Fori(0, 2) as i:
                for m in range(4):
                    b = 4 * (m % 2)
                    n = U_M + 3 * m
                    pe.wait_ge(merged_ready, 4 * i + (m + 1))
                    pe.wait_ge(lo_ready, 12 * i + (n + 1))
                    product(n % WS, b, h_rhs(h_hi), h_rhs(h_lo), range(KC))
                    pe.wait_ge(lo_ready, 12 * i + (n + 2))
                    product((n + 1) % WS, b + 1, h_rhs(h_hi), h_rhs(h_lo), range(KC))
                    pe.wait_ge(lo_ready, 12 * i + (n + 3))
                    product((n + 2) % WS, b + 2, h_rhs(oa_hi), h_rhs(oa_lo), range(0, 4))
                    product((n + 2) % WS, b + 3, h_rhs(ob_hi), h_rhs(ob_lo), range(4, 8))

            pe.wait_ge(merged_ready, KC + 2)
            pe.wait_ge(ada_used, 24)
            for j in range(4 * KC):
                end = mm(bank[2][:, j:j + 1], ada_acc2[:, j // 16, (j % 16) * P:(j % 16 + 1) * P],
                         ones[:, 0:1], start=True, stop=True)
            end.then_inc(mod_turned, 1)
            for m in range(KC):
                n = U_O + m
                g = G[n]
                pe.wait_ge(lin_evac, E_O + m - 1)
                pe.wait_ge(lo_ready, n + 1)
                product(n % WS, g % 2, h_rhs(m_hi), h_rhs(m_lo), range(KC))
                if m:
                    sum_square(11, m == 1, False, ones, sq_o)
            sum_square(11, False, True, ones, sq_o)

            pe.wait_ge(t_lo, T_U)
            for half in range(2):
                pe.wait_ge(lin_evac, E_1[half])
                with pe.Fori(0, 4) as i:
                    for j in range(4):
                        n = U_1[half] + j
                        g = G[n]
                        pe.wait_ge(lo_ready, 4 * i + (n + 1))
                        pe.wait_ge(lin_evac, 4 * i + (E_1[half] + j - 1))
                        product(n % WS, g % 2, h_rhs(h_hi), h_rhs(h_lo), range(KC))
                pe.wait_ge(t_lo, T_U + MH * (half + 1))

                def down(i, js=range(4)):
                    for j in js:
                        n = U_2[half] + j
                        pe.wait_ge(lo_ready, 4 * i + (n + 1))
                        if j % 2 == 0:
                            pe.wait_ge(lin_evac, 2 * i + (E_2[half] + j // 2 - 1))
                        off = 8 * (j % 2)
                        product(n % WS, j // 2, lambda k, o=off: u_hi[:, o + k], lambda k, o=off: u_lo[:, o + k],
                                range(8), first=j % 2 == 0, last=j % 2 == 1)

                with pe.Fori(0, 4) as i:
                    down(i)
            for m in range(KC):
                pe.wait_ge(lin_evac, E_2[1] + m + 1)
                if m >= 2:
                    pe.wait_ge(out_staged, m - 1)
                for b in range(TB):
                    end = nc.tensor.transpose(bank[2 + m % 2][:, b * P:(b + 1) * P],
                                              xT[:, m, b * P:(b + 1) * P], ident[:])
                end.then_inc(y_turned, 1)


_INS = ['x', 'c', 'w_ada', 'b_ada', 'norm1_g', 'w_in', 'q_lat_norm_g', 'w_uq', 'w_uq_idx', 'q_norm_g',
        'k_norm_g', 'k_idx_norm_g', 'hgrn_lb', 'hgrn_o_norm_g', 'w_proj_a', 'w_proj_b', 'w_out',
        'norm2_g', 'w_mlp1', 'b_mlp1', 'w_mlp2', 'b_mlp2']


def kernel(**inputs):
    import numpy as np
    import concourse.bacc as bacc
    from concourse.bass_utils import run_bass_kernel_spmd

    nc = bacc.Bacc("TRN2", target_bir_lowering=False, num_devices=1)
    arrays, args = {}, []
    for name in _INS:
        a = np.ascontiguousarray(inputs[name])
        arrays[f"in_{name}"] = a
        args.append(nc.dram_tensor(f"in_{name}", a.shape, mybir.dt.from_np(a.dtype),
                                   kind="ExternalInput").ap())
    out = nc.dram_tensor("out", inputs["x"].shape, F32, kind="ExternalOutput").ap()
    hybrid_block(nc, *args, out)
    return run_bass_kernel_spmd(nc, [arrays], core_ids=[0]).results[0]["out"]
```

```python
from contextlib import ExitStack

import concourse.bass as bass
from concourse import mybir

F32 = mybir.dt.float32
F32R = mybir.dt.float32r
I8 = mybir.dt.int8
ALU = mybir.AluOpType
ACT = mybir.ActivationFunctionType

P = 128
WS = 4
EPS = 1e-6
MASKED = -3.0e38
TAKEN = -3.4028235e38
TAKEN_BELOW = -3.3e38
FORBID = -1.0e30


def hybrid_block(nc, x, c, w_ada, b_ada, norm1_g, w_in, q_lat_norm_g, w_uq, w_uq_idx, q_norm_g,
                 k_norm_g, k_idx_norm_g, hgrn_lb, hgrn_o_norm_g, w_proj_a, w_proj_b, w_out,
                 norm2_g, w_mlp1, b_mlp1, w_mlp2, b_mlp2, out):
    T, D = x.shape[1], x.shape[2]
    KC = D // P
    TB = T // P
    R = q_lat_norm_g.shape[1]
    AW = w_proj_a.shape[1]
    HD = q_norm_g.shape[1]
    AH = AW // HD
    IH = w_uq_idx.shape[2] // HD
    BW = w_proj_b.shape[1]
    BH = BW // P
    DFF = w_mlp1.shape[2]
    TOPK = min(256, T // 4)
    RC, AC, MH = R // P, AW // P, DFF // P // 2
    assert (KC, TB, RC, AC, BH, IH, TOPK) == (8, 4, 2, 4, 4, 4, P) and 2 * HD == P and MH == 16

    C_QLAT = 0
    C_K = C_QLAT + R
    C_V = C_K + AW
    C_KIDX = C_V + AW
    C_WIDX = C_KIDX + HD
    C_B = C_WIDX + IH
    C_GA = C_B + 4 * BW
    C_GB = C_GA + D

    V_C, V_G1, V_G2, V_QG = 0, 8, 16, 24
    V_B1 = 26
    V_B2 = V_B1 + 2 * MH
    V_BADA = V_B2 + KC
    V_LB = V_BADA + 6 * KC
    V_OG = V_LB + 2 * BH
    V_HQ = V_OG + BH
    V_HK = V_HQ + 1
    assert V_HK == P - 1

    U_KIDX, U_WIDX, U_K, U_UQI, U_V, U_UQ, U_B = 2, 3, 4, 8, 9, 13, 14
    U_M = U_B + 16
    U_P = U_M + 2 * KC
    U_O = U_P + KC
    U_1 = [U_O + KC, U_O + KC + 2 * MH]
    U_2 = [u + MH for u in U_1]
    N_UNITS = U_2[1] + MH
    groups = [1] * N_UNITS
    groups[U_UQI], groups[U_UQ] = 2, 4
    for m in range(KC):
        groups[U_P + m] = 2
    G = [0]
    for g in groups:
        G.append(G[-1] + g)

    E_O = G[U_P]
    E_1 = [E_O + KC, E_O + 2 * KC + MH]
    E_2 = [e + MH for e in E_1]

    T_U = 2 * KC + RC

    w_in_v = w_in[0].rearrange("(k p) n -> p k n", p=P)
    w_uq_v = w_uq[0].rearrange("(k p) (m n) -> p k m n", p=P, n=P)
    w_uqi_v = w_uq_idx[0].rearrange("(k p) (m n) -> p k m n", p=P, n=P)
    w_pa_v = w_proj_a[0].rearrange("(k p) n -> p k n", p=P)
    w_pb_v = w_proj_b[0].rearrange("(k p) n -> p k n", p=P)
    w_out_v = w_out[0].rearrange("(k p) n -> p k n", p=P)
    w_1_v = w_mlp1[0].rearrange("(k p) n -> p k n", p=P)
    w_2_v = w_mlp2[0].rearrange("(k p) n -> p k n", p=P)
    w_ada_v = w_ada[0].rearrange("(k p) (g n) -> g k p n", p=P, g=3)
    w_ada_v2 = w_ada[0].rearrange("(k p) (g n) -> g k p n", p=P, g=6)
    out_v = out[0].rearrange("(b p) (m n) -> m p b n", p=P, n=P)

    with ExitStack() as ctx:
        base = -(-nc.sbuf_base // 32) * 32
        KB = 1024
        at = {}

        def place(name, offset, shape, dt=F32):
            at[name] = nc.alloc_sbuf_tensor_at(name, shape, dt, offset=base + offset)
            return at[name]

        w_raw = place("w_raw", 0, [P, WS, 8, P])
        w_hi = place("w_hi", 16 * KB, [P, WS, 8, P], F32R)
        w_lo = place("w_lo", 32 * KB, [P, WS, 8, P], F32R)
        xT = place("xT", 48 * KB, [P, KC, T])
        h_hi = place("h_hi", 64 * KB, [P, KC, T], F32R)
        h_lo = place("h_lo", 80 * KB, [P, KC, T], F32R)
        RB = 96 * KB
        bT = place("bT", RB, [P, 4 * BH, T])
        sig_a = place("sig_a", RB + 16 * KB, [P, KC, T])
        ada_raw = place("ada_raw", RB, [P, 4, 2048])
        rt_k = place("rt_k", RB, [P, 4, T])
        vT = place("vT", RB + 16 * KB, [P, AC, T])
        ob_hi = place("ob_hi", RB, [P, BH, T], F32R)
        ob_lo = place("ob_lo", RB + 8 * KB, [P, BH, T], F32R)
        u_hi = place("u_hi", RB, [P, MH, T], F32R)
        RA = 128 * KB
        kT = place("kT", RA, [P, AC, T])
        qT = place("qT", RA + 8 * KB, [P, AC, T])
        score = place("score", RA + 16 * KB, [P, TB, T])
        v_nat = place("v_nat", RA + 24 * KB, [P, TB, T])
        i_nat = place("i_nat", RA + 32 * KB, [P, TB, T])
        ada_acc = place("ada_acc", RA, [P, 2048])
        x_nat = place("x_nat", RA + 24 * KB, [P, TB, D])
        oa_hi = place("oa_hi", RA + 8 * KB, [P, AC, T], F32R)
        oa_lo = place("oa_lo", RA, [P, AC, T], F32R)
        u_lo = place("u_lo", RA, [P, MH, T], F32R)
        RL = 168 * KB
        latT = place("latT", RL, [P, RC, T])
        lat_hi = place("lat_hi", RL + 4 * KB, [P, RC, T], F32R)
        lat_lo = place("lat_lo", RL + 8 * KB, [P, RC, T], F32R)
        kiT = place("kiT", RL + 12 * KB, [P, T])
        wiT = place("wiT", RL + 14 * KB, [P, T])
        qiT = place("qiT", RL + 16 * KB, [P, RC, T])
        sq = place("sq", RL + 20 * KB, [P, 2, T])
        rt = place("rt", RL + 24 * KB, [P, 2, T])
        tmp = place("tmp", RL + 28 * KB, [P, 2, T])
        rel = place("rel", RL + 28 * KB, [P, 2, T])
        rt_q = place("rt_q", RL, [P, 4, T])
        pr = place("pr", RL, [P, 2, 1280])
        prT = place("prT", RL + 10 * KB, [P, 1280])
        ada_acc2 = place("ada_acc2", RL, [P, D])
        ada_raw2 = place("ada_raw2", RL + 4 * KB, [P, 2, D])
        hg_rt = place("hg_rt", RL + 12 * KB, [P, T])
        hg_e = place("hg_e", RL + 15 * KB, [P, T])
        hg_k = place("hg_k", RL + 17 * KB, [P, T])
        hg_qk = place("hg_qk", RL + 19 * KB, [P, 2, T])
        hg_at = place("hg_at", RL + 23 * KB, [P, T])
        hg_kn = place("hg_kn", RL + 25 * KB, [P, T])
        hg_s = place("hg_s", RL + 27 * KB, [P, 3, P])
        hg_t = place("hg_t", RL + 29 * KB, [P, T])
        q_sig = [hg_t, hg_kn, hg_e, hg_k]
        sig_b = place("sig_b", RL + 16 * KB, [P, KC, T])
        sq_o = place("sq_o", RA + 16 * KB, [P, 2, T])
        rt_o = place("rt_o", RA + 20 * KB, [P, T])
        relu_u = place("relu_u", RL, [P, 2, T])
        sqr_u = place("sqr_u", RL + 4 * KB, [P, 2, T])
        o_stage = place("o_stage", RL + 8 * KB, [P, 2, TB, P])
        RC_ = 200 * KB
        ident = place("ident", RC_, [P, P])
        ones = place("ones", RC_ + 512, [P, P])
        twins = place("twins", RC_ + 1024, [P, P])
        causal = place("causal", RC_ + 1536, [P, P])
        col = place("col", RC_ + 2048, [P, P])
        vec = place("vec", RC_ + 2560, [P, P])
        mod = place("mod", RC_ + 3072, [P, 6 * KC])
        sc = place("sc", RC_ + 3072 + 192, [P, 64])
        wi_nat = place("wi_nat", RC_ + 3072 + 448, [P, TB, IH])
        top8 = place("top8", RC_ + 3072 + 512, [P, 3, 8])
        smx = place("smx", RC_ + 3072 + 608, [P, 3, AH, TB])
        lvl_mask = place("lvl_mask", RC_ + 3072 + 992, [P, 7, P], I8)
        A1, LBC, OML, CS, CA, KIG = (sc[:, 0:8], sc[:, 8:12], sc[:, 12:16], sc[:, 16:24], sc[:, 24:32],
                                     sc[:, 32:33])
        EPSC = sc[:, 33:34]
        LBD = sc[:, 34:38]
        A2 = sc[:, 40:48]
        CC = sc[:, 48:56]
        SHIFT1, SCALE1, GATE1, SHIFT2, SCALE2, GATE2 = (mod[:, 8 * i:8 * i + 8] for i in range(6))

        bank = [ctx.enter_context(nc.psum_tensor(f"bank{i}", [P, T], F32)) for i in range(8)]

        def sem(name):
            return ctx.enter_context(nc.semaphore(name))

        c_loaded, cs_ready = sem("c_loaded"), sem("cs_ready")
        vec_loaded, x_loaded = sem("vec_loaded"), sem("x_loaded")
        ada_loaded = [sem(f"ada_loaded{i}") for i in range(4)]
        ada2_loaded, ada2_used = [sem(f"ada2_loaded{i}") for i in range(2)], sem("ada2_used")
        ada2_scaled = sem("ada2_scaled")
        w_loaded = [sem(f"w_loaded{i}") for i in range(WS)]
        hi_ready, lo_ready = sem("hi_ready"), sem("lo_ready")
        consts_ready, consts_step = sem("consts_ready"), sem("consts_step")
        dve_own, act_own = sem("dve_own"), sem("act_own")
        vec_turned, col_ready, lb_ready = sem("vec_turned"), sem("col_ready"), sem("lb_ready")
        x_turned, xT_ready = sem("x_turned"), sem("xT_ready")
        sq_ready, sq_summed, rt_ready, rt_used = (sem("sq_ready"), sem("sq_summed"), sem("rt_ready"),
                                                  sem("rt_used"))
        ada_used, mod_turned, mod_ready = sem("ada_used"), sem("mod_turned"), sem("mod_ready")
        t_ready, t_hi, t_lo = sem("t_ready"), sem("t_hi"), sem("t_lo")
        group_done, lin_evac = sem("group_done"), sem("lin_evac")
        wi_turned, wi_ready = sem("wi_turned"), sem("wi_ready")
        qk_normed = sem("qk_normed")
        score_done, rel_ready, rel_used = sem("score_done"), sem("rel_ready"), sem("rel_used")
        v_turned, v_ready = sem("v_turned"), sem("v_ready")
        i_turned, i_ready = sem("i_turned"), sem("i_ready")
        hg_sig, hg_gated = sem("hg_sig"), sem("hg_gated")
        lvl_ready, lvl_done, lvl_taken = sem("lvl_ready"), sem("lvl_done"), sem("lvl_taken")
        ks_ready, ks_turned, kn_ready, kv_done, s_ready, o_done = (
            sem("ks_ready"), sem("ks_turned"), sem("kn_ready"), sem("kv_done"), sem("s_ready"),
            sem("o_done"))
        osq_ready, osq_summed, ort_ready, o_ready, obhi_ready, ob_ready = (
            sem("osq_ready"), sem("osq_summed"), sem("ort_ready"), sem("o_ready"), sem("obhi_ready"),
            sem("ob_ready"))
        logit_done, logit_masked, nmax_ready, exp_done, prob_ready = (
            sem("logit_done"), sem("logit_masked"), sem("nmax_ready"), sem("exp_done"),
            sem("prob_ready"))
        prob_turned, probT_ready, pv_done, oahi_ready, oa_ready = (
            sem("prob_turned"), sem("probT_ready"), sem("pv_done"), sem("oahi_ready"), sem("oa_ready"))
        qf_ready = sem("qf_ready")
        merged_ready = sem("merged_ready")
        u_hi_ready = sem("u_hi_ready")
        y_turned, out_staged = sem("y_turned"), sem("out_staged")
        out_written = [sem("out_written0"), sem("out_written1")]

        block = ctx.enter_context(nc.Block())
        ds = bass.ds
        OFF_Q = [P * b * (b + 1) // 2 for b in range(TB)]
        OFF_K = [0, 512, 896, 1152]

        @block.sync
        def _(sp):
            for k in range(TB):
                sp.dma_start(x_nat[:, k], x[0, k * P:(k + 1) * P, :]).then_inc(x_loaded, 16)
            for k in range(KC):
                if k >= 4:
                    sp.wait_ge(ada_used, k - 3)
                sp.dma_start(ada_raw[:, k % 4], w_ada_v[0, k]).then_inc(ada_loaded[k % 4], 16)

            def load(n, slot, halves):
                if not isinstance(n, int) or n >= WS:
                    sp.wait_ge(lo_ready, n - WS + 1)
                for dst, src in halves:
                    sp.dma_start(dst, src).then_inc(w_loaded[slot], 16)

            def columns(view, slot, start, k0=0):
                return [(w_raw[:, slot, j:j + 4], view[:, k0 + j:k0 + j + 4, start]) for j in (0, 4)]

            load(0, 0, columns(w_in_v, 0, ds(C_QLAT, P)))
            load(1, 1, columns(w_in_v, 1, ds(C_QLAT + P, P)))
            load(2, 2, [(w_raw[:, 2, :, j * HD:(j + 1) * HD], w_in_v[:, :, C_KIDX:C_KIDX + HD])
                        for j in (0, 1)])
            load(3, 3, columns(w_in_v, 3, ds(C_WIDX, P)))
            for j in range(AC):
                n = U_K + j
                load(n, n % WS, columns(w_in_v, n % WS, ds(C_K + j * P, P)))
            s = U_UQI % WS
            load(U_UQI, s, [(w_raw[:, s, 4 * k:4 * k + 2], w_uqi_v[:, k]) for k in range(RC)])
            for j in range(AC):
                n = U_V + j
                load(n, n % WS, columns(w_in_v, n % WS, ds(C_V + j * P, P)))
            s = U_UQ % WS
            load(U_UQ, s, [(w_raw[:, s, 4 * k:4 * k + 4], w_uq_v[:, k]) for k in range(RC)])
            with sp.Fori(0, 4) as i:
                for j in range(4):
                    s = (U_B + j) % WS
                    load(4 * i + (U_B + j), s, columns(w_in_v, s, ds(((4 * i + j) * P + C_B), P)))
            gate_columns = [C_GA + m * P for m in range(KC)] + [C_GB + m * P for m in range(KC)]

            def load_gate(j):
                n = U_M + j
                load(n, n % WS, columns(w_in_v, n % WS, ds(gate_columns[j], P)))

            for j in range(WS):
                load_gate(j)
            for h in range(BH):
                load_gate(WS + 2 * h)
                load_gate(WS + 2 * h + 1)
                if h == 0:
                    sp.wait_ge(rt_used, 1 + 2 * AC)
                for k in range(KC):
                    i = KC * h + k
                    if i >= 2:
                        sp.wait_ge(ada2_used, i - 1)
                    sp.dma_start(ada_raw2[:, i % 2], w_ada_v2[2 + h, k]).then_inc(ada2_loaded[i % 2], 16)
            for j in range(WS + 2 * BH, 2 * KC):
                load_gate(j)
            with sp.Fori(0, 2) as i:
                for m in range(4):
                    s = (U_P + m) % WS
                    at_m = (4 * i + m) * P
                    sp.compute_val(at_m * 4)
                    load(4 * i + (U_P + m), s,
                         [(w_raw[:, s, 0:4], w_pa_v[:, :, ds(at_m, P)]),
                          (w_raw[:, s, 4:8], w_pb_v[:, :, ds(at_m, P)])])
            with sp.Fori(0, 2) as i:
                for j in range(4):
                    s = (U_O + j) % WS
                    load(4 * i + (U_O + j), s, columns(w_out_v, s, ds(((4 * i + j) * P), P)))
            for half in range(2):
                with sp.Fori(0, 4) as i:
                    for j in range(4):
                        s = (U_1[half] + j) % WS
                        load(4 * i + (U_1[half] + j), s,
                             columns(w_1_v, s, ds(((4 * i + (MH * half + j)) * P), P)))
                with sp.Fori(0, 4) as i:
                    for j in range(4):
                        s = (U_2[half] + j) % WS
                        load(4 * i + (U_2[half] + j), s,
                             columns(w_2_v, s, ds(((2 * i + j // 2) * P), P), MH * half + 8 * (j % 2)))
            for m in range(KC):
                sp.wait_ge(out_staged, m + 1)
                sp.dma_start(out_v[m], o_stage[:, m % 2]).then_inc(out_written[m % 2], 16)
            for b in range(2):
                sp.wait_ge(out_written[b], 16 * KC // 2)

        @block.gpsimd
        def _(pool):
            steps = [0]

            def step(ins):
                steps[0] += 1
                ins.then_inc(consts_step, 1)
                pool.wait_ge(consts_step, steps[0])

            step(nc.gpsimd.memset(ident[:], 0.0))
            step(nc.gpsimd.affine_select(out=ident[:], in_=ident[:], compare_op=ALU.not_equal, fill=1.0,
                                         base=0, pattern=[[-1, P]], channel_multiplier=1))
            step(nc.gpsimd.memset(ones[:], 1.0))
            step(nc.gpsimd.memset(EPSC, EPS))
            step(nc.gpsimd.memset(twins[:], 0.0))
            step(nc.gpsimd.memset(twins[0:HD, 0:HD], 1.0))
            step(nc.gpsimd.memset(twins[HD:P, HD:P], 1.0))
            step(nc.gpsimd.memset(causal[:], 0.0))
            step(nc.gpsimd.affine_select(out=causal[:], in_=causal[:], compare_op=ALU.is_ge, fill=MASKED,
                                         base=0, pattern=[[-1, P]], channel_multiplier=1))
            step(nc.gpsimd.memset(lvl_mask[:], 0.0))
            for l in range(7):
                H = 1 << l
                second = lvl_mask[:, l].rearrange("p (b two h) -> p b two h", two=2, h=H)[:, :, 1, :]
                nb = P // (2 * H)
                step(nc.gpsimd.memset(second, 1.0))
                for cm, b0, st in ((1, 0, -2 * H), (-1, H - 1, 2 * H)):
                    last = nc.gpsimd.affine_select(out=second, in_=second, compare_op=ALU.is_ge, fill=0.0,
                                                   base=b0, pattern=[[st, nb], [0, H]],
                                                   channel_multiplier=cm)
                    if l < 6 or cm > 0:
                        step(last)
            last.then_inc(consts_ready, 1)

            def split_lo(n, s):
                pool.wait_ge(hi_ready, n + 1)
                nc.gpsimd.tensor_tensor(w_lo[:, s], w_raw[:, s], w_hi[:, s].bitcast(F32),
                                        ALU.subtract).then_inc(lo_ready, 1)

            def split_range(n0, n1):
                with pool.Fori(0, (n1 - n0) // WS) as i:
                    for j in range(WS):
                        split_lo(WS * i + (n0 + j), (n0 + j) % WS)
                for n in range(n0 + (n1 - n0) // WS * WS, n1):
                    split_lo(n, n % WS)

            split_range(0, U_M + WS)
            for h in range(BH):
                for k in range(1, KC):
                    i = KC * h + k
                    pool.wait_ge(ada2_scaled, (KC - 1) * h + k)
                    pool.wait_ge(ada2_used, i)
                    nc.gpsimd.tensor_tensor(ada_acc2[:], ada_acc2[:], ada_raw2[:, i % 2],
                                            ALU.add).then_inc(ada2_used, 1)
                for j in range(2):
                    n = U_M + WS + 2 * h + j
                    split_lo(n, n % WS)
            split_range(U_M + WS + 2 * BH, N_UNITS)

        @block.scalar
        def _(act):
            own = [0]

            def step(ins):
                own[0] += 1
                ins.then_inc(act_own, 1)
                act.wait_ge(act_own, own[0])

            act.dma_start(CC, c.rearrange("a (k p) -> p (a k)", p=P), allow_slow_non_contiguous=True
                          ).then_inc(c_loaded, 16)
            rows = [(V_C, c.rearrange("a (k n) -> (a k) n", n=P)),
                    (V_G1, norm1_g.rearrange("a (k n) -> (a k) n", n=P)),
                    (V_G2, norm2_g.rearrange("a (k n) -> (a k) n", n=P)),
                    (V_QG, q_lat_norm_g.rearrange("a (k n) -> (a k) n", n=P)),
                    (V_B1, b_mlp1.rearrange("a (k n) -> (a k) n", n=P)),
                    (V_B2, b_mlp2.rearrange("a (k n) -> (a k) n", n=P)),
                    (V_BADA, b_ada.rearrange("a (k n) -> (a k) n", n=P)),
                    (V_LB, hgrn_lb.rearrange("a (k n) -> (a k) n", n=P)),
                    (V_OG, hgrn_o_norm_g.rearrange("a (k n) -> (a k) n", n=P))]
            for r0, src in rows:
                act.dma_start(vec[r0:r0 + src.shape[0], :], src).then_inc(vec_loaded, 16)
            for r0, src in ((V_HQ, q_norm_g), (V_HK, k_norm_g)):
                for j in (0, HD):
                    act.dma_start(vec[r0:r0 + 1, j:j + HD], src).then_inc(vec_loaded, 16)
            for j in (0, HD):
                act.dma_start(sc[j:j + HD, 32:33], k_idx_norm_g.rearrange("a (n o) -> (a n) o", o=1),
                              allow_slow_non_contiguous=True).then_inc(vec_loaded, 16)

            def split_hi(n, s=None):
                if s is None:
                    s = n % WS
                    act.wait_ge(w_loaded[s], 32 * (n // WS + 1))
                nc.scalar.activation(w_hi[:, s], w_raw[:, s], ACT.Copy).then_inc(hi_ready, 1)

            def take(g, dst, b=None):
                act.wait_ge(group_done, g + 1)
                nc.scalar.activation(dst, bank[g % 2][:dst.shape[0]], ACT.Copy).then_inc(lin_evac, 1)

            act.wait_ge(c_loaded, 16)
            nc.scalar.activation(CS, CC, ACT.Sigmoid).then_inc(cs_ready, 1)
            act.wait_ge(vec_turned, 1)
            nc.scalar.activation(col[:], bank[0][:, 0:P], ACT.Copy).then_inc(col_ready, 1)

            nsq = [0]

            def square(src, buf=sq):
                s = nsq[0]
                nsq[0] += 1
                if s >= 2:
                    act.wait_ge(sq_summed, s - 1)
                nc.scalar.activation(buf[:, s % 2], src, ACT.Square).then_inc(sq_ready, 1)

            for k in range(KC):
                act.wait_ge(x_turned, k + 1)
                square(bank[2 + k % 4][:])
                nc.scalar.activation(xT[:, k], bank[2 + k % 4][:], ACT.Copy).then_inc(xT_ready, 1)

            def root(j, s_last, dst, width):
                act.wait_ge(sq_summed, s_last + 1)
                nc.scalar.activation(dst, bank[6 + j % 2][:], ACT.Sqrt, scale=1.0 / width,
                                     bias=EPSC).then_inc(rt_ready, 1)

            act.wait_ge(consts_ready, 1)
            act.wait_ge(lb_ready, 1)
            nc.scalar.activation(LBC, LBC, ACT.Exp)
            nc.scalar.activation(OML, OML, ACT.Exp).then_inc(lb_ready, 1)
            root(0, 7, rt[:, 0], D)
            for n in range(WS):
                split_hi(n)
            act.wait_ge(mod_ready, 1)
            for k in range(KC):
                act.wait_ge(t_ready, k + 1)
                nc.scalar.activation(h_hi[:, k], tmp[:, k % 2], ACT.Identity,
                                     bias=SHIFT1[:, k:k + 1]).then_inc(t_hi, 1)

            take(0, latT[:, 0]); split_hi(4)
            take(1, latT[:, 1]); split_hi(5)
            act.wait_ge(lin_evac, 2)
            square(latT[:, 0]); square(latT[:, 1])
            take(2, kiT[:]); split_hi(6)
            act.wait_ge(lin_evac, 3)
            square(kiT[:])
            take(3, wiT[:]); split_hi(7)
            take(4, kT[:, 0]); split_hi(8)
            root(1, 9, rt[:, 1], R)
            for k in range(RC):
                act.wait_ge(t_ready, KC + k + 1)
                nc.scalar.activation(lat_hi[:, k], tmp[:, k % 2], ACT.Copy).then_inc(t_hi, 1)
            take(5, kT[:, 1]); split_hi(9)
            act.wait_ge(t_lo, KC)
            root(2, 10, rt[:, 0], HD)
            act.wait_ge(wi_turned, 1)
            nc.scalar.activation(wi_nat[:], bank[5][:, 0:TB * IH].rearrange("p (b h) -> p b h", b=TB),
                                 ACT.Copy).then_inc(wi_ready, 1)
            take(6, kT[:, 2]); split_hi(10)
            take(7, kT[:, 3]); split_hi(11)
            take(8, qiT[:, 0])
            take(9, qiT[:, 1]); split_hi(12)
            act.wait_ge(lin_evac, 8)
            for j in range(AC):
                square(kT[:, j])
                if j >= 1:
                    root(2 + j, 10 + j, rt_k[:, j - 1], HD)
            root(2 + AC, 10 + AC, rt_k[:, AC - 1], HD)

            nrel = [0]

            def relus(qb):
                n = (qb + 1) * P
                for h in range(IH):
                    s = nrel[0]
                    nrel[0] += 1
                    act.wait_ge(score_done, s + 1)
                    if s >= 2:
                        act.wait_ge(rel_used, s - 1)
                    nc.scalar.activation(rel[:, s % 2, 0:n], bank[2 + h][:, 0:n], ACT.Relu,
                                         scale=HD ** -0.5 * IH ** -0.5).then_inc(rel_ready, 1)

            take(10, vT[:, 0]); split_hi(13)
            relus(1)
            take(11, vT[:, 1]); split_hi(14)
            relus(2)
            take(12, vT[:, 2]); split_hi(15)
            relus(3)
            take(13, vT[:, 3]); split_hi(16)
            for j in range(AC):
                take(14 + j, qT[:, j])
            split_hi(17)
            for sb in range(TB):
                act.wait_ge(v_turned, sb + 1)
                nc.scalar.activation(v_nat[:, sb], bank[2 + sb][:], ACT.Copy).then_inc(v_ready, 1)

            act.wait_ge(rt_used, 1 + AC)

            def b_blocks(part):
                with act.Fori(0, 2) as i:
                    for j in range(4):
                        g = G[U_B] + 8 * part + j
                        act.wait_ge(group_done, 4 * i + (g + 1))
                        nc.scalar.activation(bT[:, ds(4 * i + (8 * part + j), 1)].rearrange("p o t -> p (o t)"),
                                             bank[g % 2][:], ACT.Copy).then_inc(lin_evac, 1)
                        n = U_B + 8 * part + j + WS
                        act.wait_ge(w_loaded[n % WS], 32 * i + 32 * (n // WS + 1))
                        split_hi(None, n % WS)

            b_blocks(0)
            for j in range(AC):
                square(qT[:, j])
                if j >= 1:
                    root(6 + j, 14 + j, rt_q[:, j - 1], HD)
            root(6 + AC, 14 + AC, rt_q[:, AC - 1], HD)
            act.wait_ge(lin_evac, G[U_B] + 2 * BH)
            act.wait_ge(rel_used, 3 * IH)
            for h in range(BH):
                nc.scalar.activation(q_sig[h][:], bT[:, h], ACT.Sigmoid).then_inc(hg_sig, 1)
                nc.scalar.activation(bT[:, BH + h], bT[:, BH + h], ACT.Sigmoid).then_inc(hg_sig, 1)
            b_blocks(1)

            act.wait_ge(lin_evac, G[U_M])
            for sb in range(TB):
                act.wait_ge(i_turned, sb + 1)
                nc.scalar.activation(i_nat[:, sb], bank[2 + sb][:], ACT.Copy).then_inc(i_ready, 1)
            act.wait_ge(rt_used, 1 + 2 * AC)
            act.wait_ge(qf_ready, 1)

            def gate(j, dst):
                n = U_M + j
                act.wait_ge(group_done, G[n + 1])
                b = G[n] % 2 if j < KC else 1
                nc.scalar.activation(dst, bank[b][:], ACT.Sigmoid).then_inc(lin_evac, 1)
                split_hi(n + WS)

            def head_out(h):
                act.wait_ge(o_ready, h + 1)
                nc.scalar.activation(ob_hi[:, h], hg_t[:], ACT.Copy).then_inc(obhi_ready, 1)

            def ada_scale(h, ks):
                for k in ks:
                    i = KC * h + k
                    act.wait_ge(ada2_loaded[i % 2], 16 * (i // 2 + 1))
                    if k == 0 and h:
                        act.wait_ge(mod_turned, h + 1)
                    dst = ada_acc2[:] if k == 0 else ada_raw2[:, i % 2]
                    nc.scalar.activation(dst, ada_raw2[:, i % 2], ACT.Copy, scale=CA[:, k:k + 1]
                                         ).then_inc(ada2_scaled if k else ada2_used, 1)

            for h in range(BH):
                if h >= 1:
                    head_out(h - 1)
                    act.wait_ge(ob_ready, h)
                nc.scalar.activation(hg_t[:], bT[:, 3 * BH + h], ACT.Sigmoid).then_inc(hg_sig, 1)
                ada_scale(h, (0, 1, 2, 3))
                act.wait_ge(ks_turned, h + 1)
                nc.scalar.activation(hg_kn[:], bank[6][:], ACT.Copy).then_inc(kn_ready, 1)
                gate(2 * h, sig_a[:, 2 * h])
                ada_scale(h, (4,))
                act.wait_ge(o_done, h + 1)
                nc.scalar.activation(hg_kn[:], bank[5][:], ACT.Square).then_inc(osq_ready, 1)
                act.wait_ge(osq_summed, h + 1)
                nc.scalar.activation(hg_rt[:], bank[7][:], ACT.Sqrt, scale=1.0 / P,
                                     bias=EPSC).then_inc(ort_ready, 1)
                if h < BH - 1:
                    gate(2 * h + 1, sig_a[:, 2 * h + 1])
                ada_scale(h, (5, 6, 7))
            head_out(BH - 1)
            gate(2 * BH - 1, sig_a[:, 2 * BH - 1])

            for h in range(AH + 1):
                if h < AH:
                    for qb in range(TB):
                        n = (qb + 1) * P
                        if qb == 0:
                            act.wait_ge(nmax_ready, h + 1)
                        p = pr[:, h % 2, OFF_Q[qb]:OFF_Q[qb] + n]
                        nc.scalar.activation(p, p, ACT.Exp, scale=HD ** -0.5,
                                             bias=smx[:, 1, h, qb:qb + 1],
                                             accum_out=smx[:, 2, h, qb:qb + 1]).then_inc(exp_done, 1)
                if h >= 1:
                    for kb in range(TB):
                        act.wait_ge(prob_turned, TB * (h - 1) + kb + 1)
                        if h >= 2 and kb == 0:
                            act.wait_ge(pv_done, h - 1)
                        w = T - kb * P
                        nc.scalar.activation(prT[:, OFF_K[kb]:OFF_K[kb] + w], bank[2 + kb][:, kb * P:T],
                                             ACT.Copy).then_inc(probT_ready, 1)
                    if (h - 1) % 2 == 1:
                        j = (h - 1) // 2
                        act.wait_ge(pv_done, h)
                        nc.scalar.activation(oa_hi[:, j], bank[0][:], ACT.Copy).then_inc(oahi_ready, 1)
                if h < AH:
                    if h == 0:
                        act.wait_ge(ob_ready, BH)
                    gate(KC + h, sig_b[:, h])

            with act.Fori(0, 2) as i:
                for m in range(4):
                    n = U_P + m
                    act.wait_ge(group_done, 8 * i + G[n + 1])
                    act.wait_ge(w_loaded[n % WS], 32 * i + 32 * (n // WS + 2))
                    split_hi(None, n % WS)

            for m in range(KC):
                act.wait_ge(lin_evac, E_O + m + 1)
                square(xT[:, m], sq_o)
                split_hi(U_O + m + WS)
            root(11, 26, rt_o[:], D)
            for k in range(KC):
                act.wait_ge(t_ready, KC + RC + k + 1)
                nc.scalar.activation(h_hi[:, k], tmp[:, k % 2], ACT.Identity,
                                     bias=SHIFT2[:, k:k + 1]).then_inc(t_hi, 1)

            for half in range(2):
                with act.Fori(0, 4) as i:
                    for j in range(4):
                        n = U_1[half] + j
                        act.wait_ge(group_done, 4 * i + G[n + 1])
                        act.wait_ge(t_lo, 4 * i + (T_U + MH * half + j - 1))
                        nc.scalar.activation(relu_u[:, j % 2], bank[G[n] % 2][:], ACT.Relu,
                                             bias=col[:, ds(4 * i + (V_B1 + MH * half + j), 1)]
                                             ).then_inc(lin_evac, 1)
                        act.wait_ge(lin_evac, 4 * i + (E_1[half] + j + 1))
                        nc.scalar.activation(u_hi[:, ds(4 * i + j, 1)].rearrange("p o t -> p (o t)"),
                                             relu_u[:, j % 2], ACT.Square).then_inc(u_hi_ready, 1)
                        act.wait_ge(w_loaded[n % WS], 32 * i + 32 * (n // WS + 2))
                        split_hi(None, n % WS)
                with act.Fori(0, 3 if half else 4) as i:
                    for j in range(4):
                        n = U_2[half] + j
                        act.wait_ge(group_done, 4 * i + G[n + 1])
                        act.wait_ge(w_loaded[n % WS], 32 * i + 32 * (n // WS + 2))
                        split_hi(None, n % WS)

            for m in range(KC):
                act.wait_ge(y_turned, m + 1)
                if m >= 2:
                    act.wait_ge(out_written[m % 2], 16 * (m // 2))
                nc.scalar.activation(o_stage[:, m % 2], bank[2 + m % 2][:].rearrange("p (b n) -> p b n", b=TB),
                                     ACT.Copy).then_inc(out_staged, 1)

        @block.vector
        def _(dve):
            own = [0]

            def step(ins):
                own[0] += 1
                ins.then_inc(dve_own, 1)
                dve.wait_ge(dve_own, own[0])

            v = nc.vector
            dve.wait_ge(c_loaded, 16)
            dve.wait_ge(cs_ready, 1)
            step(v.tensor_tensor(CA, CS, CC, ALU.mult))

            def ada_sum(acc, k, slot, loaded):
                dve.wait_ge(ada_loaded[slot], loaded)
                if k == 0:
                    v.tensor_scalar(acc, ada_raw[:, slot], CA[:, 0:1], None, ALU.mult).then_inc(ada_used, 1)
                else:
                    v.scalar_tensor_tensor(out=acc, in0=ada_raw[:, slot], scalar=CA[:, k:k + 1], in1=acc,
                                           op0=ALU.mult, op1=ALU.add).then_inc(ada_used, 1)

            for k in range(KC):
                if k >= 1:
                    dve.wait_ge(ada_used, k)
                ada_sum(ada_acc[:], k, k % 4, 16 * (k // 4 + 1))
                if k == 3:
                    dve.wait_ge(consts_ready, 1)
                    dve.wait_ge(col_ready, 1)
                    dve.wait_ge(vec_loaded, 16 * 15)
                    step(v.tensor_tensor(LBD, col[:, V_LB:V_LB + BH], col[:, V_LB + BH:V_LB + 2 * BH],
                                         ALU.max))
                    v.tensor_tensor(LBC, col[:, V_LB:V_LB + BH], LBD, ALU.subtract)
                    v.tensor_tensor(OML, col[:, V_LB + BH:V_LB + 2 * BH], LBD,
                                    ALU.subtract).then_inc(lb_ready, 1)
                if k == 7:
                    dve.wait_ge(rt_ready, 1)
                    step(v.reciprocal(rt[:, 0], rt[:, 0]))
            dve.wait_ge(mod_turned, 1)
            step(v.tensor_tensor(mod[:, 0:2 * KC], bank[1][:, 0:2 * KC], col[:, V_BADA:V_BADA + 2 * KC],
                                 ALU.add))
            v.scalar_tensor_tensor(out=A1, in0=SCALE1, scalar=1.0, in1=col[:, V_G1:V_G1 + KC], op0=ALU.add,
                                   op1=ALU.mult).then_inc(mod_ready, 1)
            dve.wait_ge(mod_ready, 1)

            nt = [0]

            def scaled(src, g, rr):
                s = nt[0]
                nt[0] += 1
                if s >= 2:
                    dve.wait_ge(t_lo, s - 1)
                v.scalar_tensor_tensor(out=tmp[:, s % 2], in0=src, scalar=g, in1=rr, op0=ALU.mult,
                                       op1=ALU.mult).then_inc(t_ready, 1)
                return s

            def lows(s, shift, hi, lo):
                dve.wait_ge(t_hi, s + 1)
                if shift is None:
                    v.tensor_tensor(lo, tmp[:, s % 2], hi.bitcast(F32), ALU.subtract).then_inc(t_lo, 1)
                else:
                    v.scalar_tensor_tensor(out=lo, in0=tmp[:, s % 2], scalar=shift, in1=hi.bitcast(F32),
                                           op0=ALU.add, op1=ALU.subtract).then_inc(t_lo, 1)

            def norm_split(src, gains, rr, shifts, hi, lo, n):
                prev = None
                for k in range(n + 1):
                    if k < n:
                        s = scaled(src[:, k], gains[:, k:k + 1], rr)
                    if prev is not None:
                        kk = k - 1
                        lows(prev, None if shifts is None else shifts[:, kk:kk + 1], hi[:, kk], lo[:, kk])
                    prev = s

            norm_split(xT, A1, rt[:, 0], SHIFT1, h_hi, h_lo, KC)
            dve.wait_ge(rt_ready, 2)
            step(v.reciprocal(rt[:, 1], rt[:, 1]))
            norm_split(latT, col[:, V_QG:V_QG + RC], rt[:, 1], None, lat_hi, lat_lo, RC)

            def head_norm(j, dst, g, rr):
                dve.wait_ge(rt_ready, j + 1)
                step(v.reciprocal(rr, rr))
                v.scalar_tensor_tensor(out=dst, in0=dst, scalar=g, in1=rr, op0=ALU.mult,
                                       op1=ALU.mult).then_inc(rt_used, 1)

            head_norm(2, kiT[:], KIG, rt[:, 0])
            for j in range(AC):
                head_norm(3 + j, kT[:, j], col[:, V_HK:V_HK + 1], rt_k[:, j])

            dve.wait_ge(wi_ready, 1)
            s = 0
            for qb in range(1, TB):
                n = (qb + 1) * P
                for h in range(IH):
                    dve.wait_ge(rel_ready, s + 1)
                    w = wi_nat[:, qb, h:h + 1]
                    if h == 0:
                        v.tensor_scalar(score[:, qb, 0:n], rel[:, s % 2, 0:n], w, None,
                                        ALU.mult).then_inc(rel_used, 1)
                    else:
                        dve.wait_ge(rel_used, s)
                        v.scalar_tensor_tensor(out=score[:, qb, 0:n], in0=rel[:, s % 2, 0:n], scalar=w,
                                               in1=score[:, qb, 0:n], op0=ALU.mult,
                                               op1=ALU.add).then_inc(rel_used, 1)
                    s += 1
                dve.wait_ge(rel_used, s)
                diag = score[:, qb, qb * P:n]
                step(v.tensor_tensor(diag, diag, causal[:], ALU.add))
            base_own = own[0]
            assert base_own >= 2
            for i in range(TOPK // 8):
                for r in range(2):
                    for qb in range(1, TB):
                        n = (qb + 1) * P
                        dve.wait_ge(dve_own, base_own + 6 * i + 3 * r + qb - 3)
                        if r == 0:
                            v.max(top8[:, qb - 1], score[:, qb, 0:n]).then_inc(dve_own, 1)
                        else:
                            v.match_replace(score[:, qb, 0:n], top8[:, qb - 1], score[:, qb, 0:n],
                                            TAKEN).then_inc(dve_own, 1)
            own[0] += 6 * (TOPK // 8)
            dve.wait_ge(dve_own, own[0])
            for qb in range(1, TB):
                n = (qb + 1) * P
                v.tensor_scalar(score[:, qb, 0:n], score[:, qb, 0:n], TAKEN_BELOW, FORBID, ALU.is_gt,
                                ALU.mult)
            step(v.tensor_scalar(score[:, 0, 0:P], causal[:], 0.0, FORBID, ALU.is_lt, ALU.mult))

            for j in range(AC):
                head_norm(7 + j, qT[:, j], col[:, V_HQ:V_HQ + 1], rt_q[:, j])

            dve.wait_ge(lb_ready, 2)
            step(v.tensor_tensor(LBD, LBC, OML, ALU.add))
            step(v.reciprocal(LBD, LBD))
            v.tensor_tensor(LBC, LBC, LBD, ALU.mult)
            step(v.tensor_tensor(OML, OML, LBD, ALU.mult))
            for h in range(BH):
                q, f = bT[:, h], bT[:, BH + h]
                dve.wait_ge(hg_sig, 2 * h + 1)
                v.tensor_tensor(q, q, q_sig[h][:], ALU.mult)
                dve.wait_ge(hg_sig, 2 * h + 2)
                last = v.tensor_scalar(f, f, OML[:, h:h + 1], LBC[:, h:h + 1], ALU.mult, ALU.add)
            last.then_inc(qf_ready, 1)
            dve.wait_ge(qf_ready, 1)

            def head_out(h):
                dve.wait_ge(ort_ready, h + 1)
                step(v.reciprocal(hg_rt[:], hg_rt[:]))
                dve.wait_ge(hg_gated, h + 1)
                step(v.scalar_tensor_tensor(out=hg_t[:], in0=bank[5][:], scalar=col[:, V_OG + h:V_OG + h + 1],
                                            in1=hg_rt[:], op0=ALU.mult, op1=ALU.mult))
                v.tensor_tensor(hg_t[:], hg_t[:], bT[:, 3 * BH + h], ALU.mult).then_inc(o_ready, 1)

            def head_out_lo(h):
                dve.wait_ge(obhi_ready, h + 1)
                v.tensor_tensor(ob_lo[:, h], hg_t[:], ob_hi[:, h].bitcast(F32),
                                ALU.subtract).then_inc(ob_ready, 1)

            for h in range(BH):
                q, f, g = bT[:, h], bT[:, BH + h], bT[:, 3 * BH + h]
                if h:
                    dve.wait_ge(ks_turned, h)
                v.tensor_scalar(hg_k[:], f, -1.0, 1.0, ALU.mult, ALU.add).then_inc(lvl_ready, 1)
                dve.wait_ge(lvl_ready, 8 * h + 1)
                step(v.memset(hg_e[:], 1.0))

                def taken(l):
                    dve.wait_ge(lvl_done, 8 * h + l + 2)
                    if l < 0 and h:
                        dve.wait_ge(o_done, h)
                    src = bank[2 + (l + 1) % 2][:].rearrange("p (b t) -> p b t", b=TB)
                    dst = hg_at[:].rearrange("p (b t) -> p b t", b=TB)
                    if l < 0:
                        v.tensor_tensor(dst, src, ident[:].unsqueeze(1).to_broadcast([P, TB, P]),
                                        ALU.mult).then_inc(lvl_taken, 1)
                    else:
                        dve.wait_ge(lvl_taken, 8 * h + l + 1)
                        v.copy_predicated(dst, lvl_mask[:, l].unsqueeze(1).to_broadcast([P, TB, P]),
                                          src).then_inc(lvl_taken, 1)

                for l in range(7):
                    H = 1 << l

                    def halves(t):
                        w = t.rearrange("p (b two h) -> p b two h", two=2, h=H)
                        return w[:, :, 0, :], w[:, :, 1, :]

                    (k1, _), (_, q2), (e1, _), (f1, f2) = (halves(hg_k[:]), halves(q), halves(hg_e[:]),
                                                           halves(f))
                    d1, d2 = halves(hg_qk[:, l % 2])
                    shape = [P, T // (2 * H), H]
                    if l >= 2:
                        dve.wait_ge(lvl_done, 8 * h + l)
                    v.tensor_tensor(d2, q2, f2, ALU.mult)
                    v.tensor_tensor(d1, k1, e1, ALU.mult).then_inc(lvl_ready, 1)
                    step(v.tensor_tensor(e1, e1, f2[:, :, H - 1:H].to_broadcast(shape), ALU.mult))
                    step(v.tensor_tensor(f2, f2, f1[:, :, H - 1:H].to_broadcast(shape), ALU.mult))
                    taken(l - 1)
                    if l == 2 and h:
                        head_out(h - 1)
                    if l == 3 and h:
                        head_out_lo(h - 1)
                    if l == 6:
                        dve.wait_ge(hg_sig, 2 * BH + h + 1)
                        v.tensor_tensor(g, g, hg_t[:], ALU.mult).then_inc(hg_gated, 1)
                taken(6)
                dve.wait_ge(lvl_done, 8 * h + 8)
                v.tensor_tensor(hg_k[:], hg_k[:], hg_e[:], ALU.mult).then_inc(ks_ready, 1)
                step(v.tensor_tensor(q, q, f, ALU.mult))
                for b in range(TB - 1):
                    dve.wait_ge(kv_done, (TB - 1) * (h + 1))
                    kv = bank[4][:, b * P:(b + 1) * P]
                    if b == 0:
                        v.tensor_copy(hg_s[:, 0], kv).then_inc(s_ready, 1)
                    else:
                        dve.wait_ge(s_ready, (TB - 1) * h + b)
                        v.scalar_tensor_tensor(out=hg_s[:, b], in0=hg_s[:, b - 1],
                                               scalar=f[:, (b + 1) * P - 1:(b + 1) * P], in1=kv,
                                               op0=ALU.mult, op1=ALU.add).then_inc(s_ready, 1)
            head_out(BH - 1)
            head_out_lo(BH - 1)
            dve.wait_ge(mod_turned, 1 + BH)
            step(v.tensor_tensor(mod[:, 2 * KC:], bank[4][:, (TB - 1) * P:(TB - 1) * P + 4 * KC],
                                 col[:, V_BADA + 2 * KC:V_BADA + 6 * KC], ALU.add))
            v.scalar_tensor_tensor(out=A2, in0=SCALE2, scalar=1.0, in1=col[:, V_G2:V_G2 + KC], op0=ALU.add,
                                   op1=ALU.mult).then_inc(mod_ready, 1)

            for h in range(AH + 1):
                if h < AH:
                    for qb in range(TB):
                        i = TB * h + qb
                        n = (qb + 1) * P
                        dve.wait_ge(logit_done, i + 1)
                        if h >= 2 and qb == 0:
                            dve.wait_ge(prob_turned, TB * (h - 1))
                        v.tensor_tensor_reduce(
                            out=pr[:, h % 2, OFF_Q[qb]:OFF_Q[qb] + n], in0=bank[6 + i % 2][:, 0:n],
                            in1=score[:, qb, 0:n], scale=1.0, scalar=TAKEN, op0=ALU.add, op1=ALU.max,
                            accum_out=smx[:, 0, h, qb:qb + 1]).then_inc(logit_masked, 1)
                    dve.wait_ge(logit_masked, TB * (h + 1))
                    v.tensor_scalar(smx[:, 1, h], smx[:, 0, h], -(HD ** -0.5), None,
                                    ALU.mult).then_inc(nmax_ready, 1)
                if h >= 2 and h % 2 == 0:
                    j = h // 2 - 1
                    dve.wait_ge(oahi_ready, j + 1)
                    v.tensor_tensor(oa_lo[:, j], bank[0][:], oa_hi[:, j].bitcast(F32),
                                    ALU.subtract).then_inc(oa_ready if j < 2 else merged_ready, 1)
                if h < AH:
                    dve.wait_ge(exp_done, TB * (h + 1))
                    step(v.reciprocal(smx[:, 2, h], smx[:, 2, h]))
                    for qb in range(TB):
                        p = pr[:, h % 2, OFF_Q[qb]:OFF_Q[qb] + (qb + 1) * P]
                        v.tensor_scalar(p, p, smx[:, 2, h, qb:qb + 1], None,
                                        ALU.mult).then_inc(prob_ready, 1)

            dve.wait_ge(lin_evac, E_O)
            with dve.Fori(0, 2) as i:
                for m in range(4):
                    dve.wait_ge(group_done, 8 * i + G[U_P + m + 1])
                    b = 4 * (m % 2)
                    own0 = own[0] + 4 * m

                    def block_m(t):
                        return t[:, ds(4 * i + m, 1)].rearrange("p o t -> p (o t)")

                    sa, sb, mh, ml = block_m(sig_a), block_m(sig_b), block_m(h_hi), block_m(h_lo)
                    v.tensor_tensor(sa, bank[b + 2][:], sa, ALU.mult).then_inc(dve_own, 1)
                    v.tensor_tensor(sb, bank[b + 3][:], sb, ALU.mult).then_inc(dve_own, 1)
                    dve.wait_ge(dve_own, 16 * i + (own0 + 2))
                    v.tensor_tensor(sa, sa, sb, ALU.add).then_inc(dve_own, 1)
                    dve.wait_ge(dve_own, 16 * i + (own0 + 3))
                    v.tensor_copy(mh, sa).then_inc(dve_own, 1)
                    dve.wait_ge(dve_own, 16 * i + (own0 + 4))
                    v.tensor_tensor(ml, sa, mh.bitcast(F32), ALU.subtract).then_inc(merged_ready, 1)
            own[0] += 32
            dve.wait_ge(mod_ready, 2)
            for m in range(KC):
                g = G[U_O + m]
                dve.wait_ge(group_done, g + 1)
                v.scalar_tensor_tensor(out=xT[:, m], in0=bank[g % 2][:], scalar=GATE1[:, m:m + 1],
                                       in1=xT[:, m], op0=ALU.mult, op1=ALU.add).then_inc(lin_evac, 1)
            dve.wait_ge(rt_ready, 12)
            step(v.reciprocal(rt_o[:], rt_o[:]))
            norm_split(xT, A2, rt_o[:], SHIFT2, h_hi, h_lo, KC)
            dve.wait_ge(t_lo, 2 * KC + RC)

            for half in range(2):
                with dve.Fori(0, 4) as i:
                    for j in range(4):
                        own0 = own[0] + j
                        dve.wait_ge(lin_evac, 4 * i + (E_1[half] + j + 1))
                        v.tensor_tensor(sqr_u[:, j % 2], relu_u[:, j % 2], relu_u[:, j % 2],
                                        ALU.mult).then_inc(dve_own, 1)
                        dve.wait_ge(dve_own, 4 * i + (own0 + 1))
                        dve.wait_ge(u_hi_ready, 4 * i + (16 * half + j + 1))
                        v.tensor_tensor(u_lo[:, ds(4 * i + j, 1)].rearrange("p o t -> p (o t)"),
                                        sqr_u[:, j % 2],
                                        u_hi[:, ds(4 * i + j, 1)].rearrange("p o t -> p (o t)").bitcast(F32),
                                        ALU.subtract).then_inc(t_lo, 1)
                own[0] += 16
                for m in range(KC):
                    dve.wait_ge(group_done, G[U_2[half]] + 2 * m + 2)
                    if half == 0:
                        step(v.tensor_scalar(sqr_u[:, m % 2], bank[m % 2][:],
                                             col[:, V_B2 + m:V_B2 + m + 1], GATE2[:, m:m + 1], ALU.add,
                                             ALU.mult))
                        v.tensor_tensor(xT[:, m], xT[:, m], sqr_u[:, m % 2], ALU.add).then_inc(lin_evac, 1)
                    else:
                        dve.wait_ge(lin_evac, E_2[0] + KC)
                        v.scalar_tensor_tensor(out=xT[:, m], in0=bank[m % 2][:], scalar=GATE2[:, m:m + 1],
                                               in1=xT[:, m], op0=ALU.mult, op1=ALU.add).then_inc(lin_evac, 1)

        @block.tensor
        def _(pe):
            mm = nc.tensor.matmul

            def product(slot, b, rhs_hi, rhs_lo, js, first=True, last=True, before=None):
                n = len(js)
                for i, j in enumerate(js):
                    if before:
                        before(i)
                    f, l = first and i == 0, last and i == n - 1
                    mm(bank[b][:], w_hi[:, slot, j], rhs_hi(i), start=f, stop=False)
                    mm(bank[b][:], w_hi[:, slot, j], rhs_lo(i), start=False, stop=False)
                    end = mm(bank[b][:], w_lo[:, slot, j], rhs_hi(i), start=False, stop=l)
                end.then_inc(group_done, 1)

            def h_rhs(t):
                return lambda k: t[:, k]

            def unit(n, before=None):
                g = G[n]
                pe.wait_ge(lo_ready, n + 1)
                if g >= 2:
                    pe.wait_ge(lin_evac, g - 1)
                product(n % WS, g % 2, h_rhs(h_hi), h_rhs(h_lo), range(KC), before=before)

            pe.wait_ge(consts_ready, 1)
            pe.wait_ge(vec_loaded, 16 * 15)
            nc.tensor.transpose(bank[0][:, 0:P], vec[:], ident[:]).then_inc(vec_turned, 1)
            ns = [0]

            def sum_square(j, first, last, ones_, buf=sq):
                s = ns[0]
                ns[0] += 1
                pe.wait_ge(sq_ready, s + 1)
                if first and j >= 2:
                    pe.wait_ge(rt_ready, j - 1)
                mm(bank[6 + j % 2][:], ones_[:], buf[:, s % 2], start=first, stop=last
                   ).then_inc(sq_summed, 1)

            def sum_squares(j, n, ones_):
                for i in range(n):
                    sum_square(j, i == 0, i == n - 1, ones_)

            pe.wait_ge(x_loaded, 16 * TB)
            for k in range(KC):
                if k >= 4:
                    pe.wait_ge(xT_ready, k - 3)
                for b in range(TB):
                    end = nc.tensor.transpose(bank[2 + k % 4][:, b * P:(b + 1) * P],
                                              x_nat[:, b, k * P:(k + 1) * P], ident[:])
                end.then_inc(x_turned, 1)
                if k:
                    sum_square(0, k == 1, False, ones)
            sum_square(0, False, True, ones)
            pe.wait_ge(ada_used, KC)
            for j in range(2 * KC):
                end = mm(bank[1][:, j:j + 1], ada_acc[:, j * P:(j + 1) * P], ones[:, 0:1], start=True,
                         stop=True)
            end.then_inc(mod_turned, 1)
            pe.wait_ge(mod_ready, 1)
            unit(0, before=lambda k: pe.wait_ge(t_lo, k + 1))
            for n in (1, 2, 3, 4):
                unit(n)
            sum_squares(1, RC, ones)
            unit(5)
            sum_squares(2, 1, twins)
            for b in range(TB):
                end = nc.tensor.transpose(bank[5][:, b * IH:(b + 1) * IH], wiT[0:IH, b * P:(b + 1) * P],
                                          ident[0:IH, 0:IH])
            end.then_inc(wi_turned, 1)
            unit(6)
            unit(7)
            pe.wait_ge(lo_ready, U_UQI + 1)
            pe.wait_ge(t_lo, KC + RC)
            for m in range(2):
                g = G[U_UQI] + m
                pe.wait_ge(lin_evac, g - 1)
                product(U_UQI % WS, g % 2, h_rhs(lat_hi), h_rhs(lat_lo), [4 * k + m for k in range(RC)])
            for j in range(AC):
                sum_squares(3 + j, 1, twins)
            nscore = [0]

            def scores(qb):
                n = (qb + 1) * P
                for h in range(IH):
                    r = HD * (h % 2)
                    s = nscore[0]
                    nscore[0] += 1
                    if s >= IH:
                        pe.wait_ge(rel_ready, s - IH + 1)
                    mm(bank[2 + h][:, 0:n], qiT[r:r + HD, h // 2, qb * P:(qb + 1) * P], kiT[r:r + HD, 0:n],
                       start=True, stop=True).then_inc(score_done, 1)

            unit(9)
            pe.wait_ge(lin_evac, 10)
            pe.wait_ge(rt_used, 1)
            pe.wait_ge(wi_ready, 1)
            scores(1)
            unit(10)
            scores(2)
            unit(11)
            scores(3)
            unit(12)
            pe.wait_ge(lo_ready, U_UQ + 1)
            for m in range(AC):
                g = G[U_UQ] + m
                pe.wait_ge(lin_evac, g - 1)
                product(U_UQ % WS, g % 2, h_rhs(lat_hi), h_rhs(lat_lo), [4 * k + m for k in range(RC)])
            pe.wait_ge(rel_ready, 3 * IH)
            for sb in range(TB):
                for j in range(AC):
                    end = nc.tensor.transpose(bank[2 + sb][:, j * P:(j + 1) * P], vT[:, j, sb * P:(sb + 1) * P],
                                              ident[:])
                end.then_inc(v_turned, 1)

            def b_blocks(part):
                with pe.Fori(0, 2) as i:
                    for j in range(4):
                        n = U_B + 8 * part + j
                        g = G[n]
                        pe.wait_ge(lo_ready, 4 * i + (n + 1))
                        pe.wait_ge(lin_evac, 4 * i + (g - 1))
                        product(n % WS, g % 2, h_rhs(h_hi), h_rhs(h_lo), range(KC))

            b_blocks(0)
            for j in range(AC):
                sum_squares(7 + j, 1, twins)
            b_blocks(1)

            pe.wait_ge(lin_evac, G[U_M])
            pe.wait_ge(v_ready, TB)
            pe.wait_ge(rt_ready, 11)
            for sb in range(TB):
                for j in range(BH):
                    end = nc.tensor.transpose(bank[2 + sb][:, j * P:(j + 1) * P],
                                              bT[:, 2 * BH + j, sb * P:(sb + 1) * P], ident[:])
                end.then_inc(i_turned, 1)
            pe.wait_ge(i_ready, TB)

            def gate_blocks(j, k0, k1):
                n = U_M + j
                b = G[n] % 2 if j < KC else 1
                if k0 == 0:
                    pe.wait_ge(lo_ready, n + 1)
                    pe.wait_ge(lin_evac, G[n] - 1 if j < KC else G[n])
                for k in range(k0, k1):
                    mm(bank[b][:], w_hi[:, n % WS, k], h_hi[:, k], start=k == 0, stop=False)
                    mm(bank[b][:], w_hi[:, n % WS, k], h_lo[:, k], start=False, stop=False)
                    end = mm(bank[b][:], w_lo[:, n % WS, k], h_hi[:, k], start=False, stop=k == KC - 1)
                if k1 == KC:
                    end.then_inc(group_done, 1)

            def mod_columns(h):
                pe.wait_ge(ada2_used, KC * (h + 1))
                for j in range(KC):
                    at_j = (TB - 1) * P + KC * h + j
                    end = mm(bank[4][:, at_j:at_j + 1], ada_acc2[:, j * P:(j + 1) * P], ones[:, 0:1],
                             start=True, stop=True)
                end.then_inc(mod_turned, 1)

            pe.wait_ge(qf_ready, 1)
            for h in range(BH):
                q = bT[:, h]
                for l in range(-1, 7):
                    pe.wait_ge(lvl_ready, 8 * h + l + 2)
                    if h or l >= 1:
                        pe.wait_ge(lvl_taken, 8 * h + l)
                    for b in range(TB):
                        t = slice(b * P, (b + 1) * P)
                        lhs, rhs = (hg_k[:, t], q[:, t]) if l < 0 else (hg_qk[:, l % 2, t], hg_qk[:, l % 2, t])
                        end = mm(bank[2 + (l + 1) % 2][:, t], lhs, rhs, start=True, stop=True)
                    end.then_inc(lvl_done, 1)
                    if l == 1 and h:
                        mod_columns(h - 1)
                    if l >= 1:
                        gate_blocks(2 * h, l - 1, l)
                pe.wait_ge(ks_ready, h + 1)
                if h:
                    pe.wait_ge(kn_ready, h)
                for b in range(TB):
                    t = slice(b * P, (b + 1) * P)
                    end = nc.tensor.transpose(bank[6][:, t], hg_k[:, t], ident[:])
                end.then_inc(ks_turned, 1)
                gate_blocks(2 * h, 6, 8)
                pe.wait_ge(kn_ready, h + 1)
                if h:
                    pe.wait_ge(s_ready, (TB - 1) * h)
                for b in range(TB - 1):
                    t = slice(b * P, (b + 1) * P)
                    mm(bank[4][:, t], hg_kn[:, t], i_nat[:, b, h * P:(h + 1) * P], start=True,
                       stop=True).then_inc(kv_done, 1)
                gate_blocks(2 * h + 1, 0, 2)
                pe.wait_ge(lvl_taken, 8 * h + 8)
                pe.wait_ge(s_ready, (TB - 1) * (h + 1))
                if h:
                    pe.wait_ge(o_ready, h)
                for b in range(TB):
                    t = slice(b * P, (b + 1) * P)
                    end = mm(bank[5][:, t], i_nat[:, b, h * P:(h + 1) * P], hg_at[:, t], start=True,
                             stop=b == 0)
                    if b:
                        end = mm(bank[5][:, t], hg_s[:, b - 1], q[:, t], start=False, stop=True)
                end.then_inc(o_done, 1)
                gate_blocks(2 * h + 1, 2, 4)
                pe.wait_ge(osq_ready, h + 1)
                if h:
                    pe.wait_ge(ort_ready, h)
                mm(bank[7][:], ones[:], hg_kn[:], start=True, stop=True).then_inc(osq_summed, 1)
                gate_blocks(2 * h + 1, 4, 8)
            mod_columns(BH - 1)

            pe.wait_ge(ort_ready, BH)
            for h in range(AH + 1):
                if h < AH:
                    r = HD * (h % 2)
                    for qb in range(TB):
                        i = TB * h + qb
                        n = (qb + 1) * P
                        if i >= 2:
                            pe.wait_ge(logit_masked, i - 1)
                        mm(bank[6 + i % 2][:, 0:n], qT[r:r + HD, h // 2, qb * P:(qb + 1) * P],
                           kT[r:r + HD, h // 2, 0:n], start=True, stop=True).then_inc(logit_done, 1)
                    gate_blocks(KC + h, 0, 4)
                if h >= 1:
                    g = h - 1
                    r = HD * (g % 2)
                    j = g // 2
                    for kb in range(TB):
                        if g:
                            pe.wait_ge(probT_ready, TB * (g - 1) + kb + 1)
                        for qb in range(kb, TB):
                            pe.wait_ge(prob_ready, TB * g + qb + 1)
                            o = OFF_Q[qb] + kb * P
                            end = nc.tensor.transpose(bank[2 + kb][:, qb * P:(qb + 1) * P],
                                                      pr[:, g % 2, o:o + P], ident[:])
                        end.then_inc(prob_turned, 1)
                    if h < AH:
                        gate_blocks(KC + h, 4, 8)
                    if g == 2 or g == 4:
                        pe.wait_ge(oa_ready, j)
                    if g == 6:
                        pe.wait_ge(merged_ready, 1)
                    for kb in range(TB):
                        pe.wait_ge(probT_ready, TB * g + kb + 1)
                        w = T - kb * P
                        end = mm(bank[0][r:r + HD, kb * P:T], v_nat[:, kb, g * HD:(g + 1) * HD],
                                 prT[:, OFF_K[kb]:OFF_K[kb] + w], start=kb == 0, stop=kb == TB - 1)
                    end.then_inc(pv_done, 1)
                else:
                    gate_blocks(KC + h, 4, 8)

            pe.wait_ge(merged_ready, 2)
            with pe.Fori(0, 2) as i:
                for m in range(4):
                    b = 4 * (m % 2)
                    n = U_P + m
                    pe.wait_ge(merged_ready, 4 * i + (m + 1))
                    pe.wait_ge(lo_ready, 4 * i + (n + 1))
                    product(n % WS, b + 2, h_rhs(oa_hi), h_rhs(oa_lo), range(0, 4))
                    product(n % WS, b + 3, h_rhs(ob_hi), h_rhs(ob_lo), range(4, 8))

            pe.wait_ge(merged_ready, KC + 2)
            for m in range(KC):
                n = U_O + m
                g = G[n]
                pe.wait_ge(lin_evac, E_O + m - 1)
                pe.wait_ge(lo_ready, n + 1)
                product(n % WS, g % 2, h_rhs(h_hi), h_rhs(h_lo), range(KC))
                if m:
                    sum_square(11, m == 1, False, ones, sq_o)
            sum_square(11, False, True, ones, sq_o)

            for half in range(2):
                pe.wait_ge(lin_evac, E_1[half])
                with pe.Fori(0, 4) as i:
                    for j in range(4):
                        n = U_1[half] + j
                        g = G[n]
                        pe.wait_ge(lo_ready, 4 * i + (n + 1))
                        pe.wait_ge(lin_evac, 4 * i + (E_1[half] + j - 1))
                        product(n % WS, g % 2, h_rhs(h_hi), h_rhs(h_lo), range(KC),
                                before=(lambda k: pe.wait_ge(t_lo, T_U - KC + k + 1))
                                if half == 0 and j == 0 else None)
                pe.wait_ge(t_lo, T_U + MH * (half + 1))

                def down(i, js=range(4)):
                    for j in js:
                        n = U_2[half] + j
                        pe.wait_ge(lo_ready, 4 * i + (n + 1))
                        if j % 2 == 0:
                            pe.wait_ge(lin_evac, 2 * i + (E_2[half] + j // 2 - 1))
                        off = 8 * (j % 2)
                        product(n % WS, j // 2, lambda k, o=off: u_hi[:, o + k], lambda k, o=off: u_lo[:, o + k],
                                range(8), first=j % 2 == 0, last=j % 2 == 1)

                with pe.Fori(0, 4) as i:
                    down(i)
            for m in range(KC):
                pe.wait_ge(lin_evac, E_2[1] + m + 1)
                if m >= 2:
                    pe.wait_ge(out_staged, m - 1)
                for b in range(TB):
                    end = nc.tensor.transpose(bank[2 + m % 2][:, b * P:(b + 1) * P],
                                              xT[:, m, b * P:(b + 1) * P], ident[:])
                end.then_inc(y_turned, 1)


_INS = ['x', 'c', 'w_ada', 'b_ada', 'norm1_g', 'w_in', 'q_lat_norm_g', 'w_uq', 'w_uq_idx', 'q_norm_g',
        'k_norm_g', 'k_idx_norm_g', 'hgrn_lb', 'hgrn_o_norm_g', 'w_proj_a', 'w_proj_b', 'w_out',
        'norm2_g', 'w_mlp1', 'b_mlp1', 'w_mlp2', 'b_mlp2']


def kernel(**inputs):
    import numpy as np
    import concourse.bacc as bacc
    from concourse.bass_utils import run_bass_kernel_spmd

    nc = bacc.Bacc("TRN2", target_bir_lowering=False, num_devices=1)
    arrays, args = {}, []
    for name in _INS:
        a = np.ascontiguousarray(inputs[name])
        arrays[f"in_{name}"] = a
        args.append(nc.dram_tensor(f"in_{name}", a.shape, mybir.dt.from_np(a.dtype),
                                   kind="ExternalInput").ap())
    out = nc.dram_tensor("out", inputs["x"].shape, F32, kind="ExternalOutput").ap()
    hybrid_block(nc, *args, out)
    return run_bass_kernel_spmd(nc, [arrays], core_ids=[0]).results[0]["out"]
```
